# Optimizing a Trainium2 kernel written in Bass

```python
import math
import jax, jax.numpy as jnp
from jax import lax
import numpy as np

D_MODEL = 1024
BATCH = 1
SEQ = 256
DEPTH = 2

CTX_LEN = 256
GRID_W = 64
DIFF_HEADS = 4
DIFF_HD = 64
DIFF_VD = 2 * DIFF_HD
MLA_HEADS = 8
MLA_NOPE = 64
MLA_ROPE = 32
MLA_VD = 64
MLA_Q_RANK = 384
MLA_KV_RANK = 256
FOURIER_GROUPS = 4
FOURIER_GROUP_DIM = 128
N_BRANCHES = 3
D_FF = 2816
Q_BLOCK = 128
ROPE_BASE = 10000.0
RMS_EPS = 1e-6
N_MOD = 9

DIFF_Q_W = DIFF_HEADS * 2 * DIFF_HD
DIFF_V_W = DIFF_HEADS * DIFF_VD
FOURIER_W = FOURIER_GROUPS * FOURIER_GROUP_DIM
MLA_OUT_W = MLA_HEADS * MLA_VD
IN_SIZES = (DIFF_Q_W, DIFF_Q_W, DIFF_V_W, MLA_Q_RANK, MLA_KV_RANK, MLA_ROPE, FOURIER_W, N_BRANCHES * D_MODEL)
IN_WIDTH = sum(IN_SIZES)

kernel_name = 'hybrid_diff_mla_fourier_macaron_dit'

def rms_norm(x, g):
    x32 = x.astype(jnp.float32)
    y = x32 * lax.rsqrt(jnp.mean(x32 * x32, axis=-1, keepdims=True) + RMS_EPS)
    return (y * g.astype(jnp.float32)).astype(x.dtype)

def modulate(x, shift, scale):
    return x * (1 + scale) + shift

def swiglu(x, w_in, w_out):
    g, u = jnp.split(x @ w_in, 2, axis=-1)
    return (jax.nn.silu(g) * u) @ w_out

def axial_rope_tables(row, col, dim):
    nf = dim // 4
    freqs = jnp.power(ROPE_BASE, -jnp.arange(nf, dtype=jnp.float32) / nf)
    ar = row.astype(jnp.float32)[:, None] * freqs[None, :]
    ac = col.astype(jnp.float32)[:, None] * freqs[None, :]
    ang = jnp.concatenate([ar, ar, ac, ac], axis=-1)
    return jnp.cos(ang), jnp.sin(ang)

def axial_rope(x, cos, sin):
    x1, x2, x3, x4 = jnp.split(x, 4, axis=-1)
    rot = jnp.concatenate([-x2, x1, -x4, x3], axis=-1)
    return (x * cos + rot * sin).astype(x.dtype)

def sweep_query_blocks(fn, qs):
    b, h, n, _ = qs[0].shape
    nb = n // Q_BLOCK
    blocks = tuple(q.reshape(b, h, nb, Q_BLOCK, q.shape[-1]).transpose(2, 0, 1, 3, 4) for q in qs)
    out = lax.map(lambda qb: fn(*qb), blocks)
    return out.transpose(1, 2, 0, 3, 4).reshape(b, h, n, out.shape[-1])

def diff_attend(q1, q2, k1, k2, v, lam):
    scale = DIFF_HD ** -0.5
    p1 = jax.nn.softmax(jnp.einsum('bhqd,bhkd->bhqk', q1, k1).astype(jnp.float32) * scale, axis=-1)
    p2 = jax.nn.softmax(jnp.einsum('bhqd,bhkd->bhqk', q2, k2).astype(jnp.float32) * scale, axis=-1)
    w = p1 - lam.astype(jnp.float32) * p2
    return jnp.einsum('bhqk,bhkv->bhqv', w.astype(v.dtype), v)

def mla_attend(qn, qr, kn, kr, v):
    scale = (MLA_NOPE + MLA_ROPE) ** -0.5
    s = jnp.einsum('bhqd,bhkd->bhqk', qn, kn) + jnp.einsum('bhqr,bkr->bhqk', qr, kr)
    p = jax.nn.softmax(s.astype(jnp.float32) * scale, axis=-1)
    return jnp.einsum('bhqk,bhkv->bhqv', p.astype(v.dtype), v)

def split_heads(t, heads, dim):
    b, n, _ = t.shape
    return t.reshape(b, n, heads, dim).transpose(0, 2, 1, 3)

def merge_heads(t):
    b, h, n, d = t.shape
    return t.transpose(0, 2, 1, 3).reshape(b, n, h * d)

def split_proj(p):
    offsets = []
    acc = 0
    for s in IN_SIZES[:-1]:
        acc += s
        offsets.append(acc)
    return jnp.split(p, offsets, axis=-1)

def diff_qkv(pq, pk, pv):
    b, n, _ = pq.shape
    q = pq.reshape(b, n, DIFF_HEADS, 2, DIFF_HD).transpose(3, 0, 2, 1, 4)
    k = pk.reshape(b, n, DIFF_HEADS, 2, DIFF_HD).transpose(3, 0, 2, 1, 4)
    v = split_heads(pv, DIFF_HEADS, DIFF_VD)
    return q[0], q[1], k[0], k[1], v

def diff_out(o, subln_g, lam_init):
    return merge_heads(rms_norm(o, subln_g) * (1.0 - lam_init))

def mla_qkv(pcq, pckv, q_norm_g, w_uq, kv_norm_g, w_ukv):
    q = split_heads(rms_norm(pcq, q_norm_g) @ w_uq, MLA_HEADS, MLA_NOPE + MLA_ROPE)
    kv = split_heads(rms_norm(pckv, kv_norm_g) @ w_ukv, MLA_HEADS, MLA_NOPE + MLA_VD)
    return q[..., :MLA_NOPE], q[..., MLA_NOPE:], kv[..., :MLA_NOPE], kv[..., MLA_NOPE:]

def fourier_mix(pf):
    b, n, _ = pf.shape
    f = pf.reshape(b, n, FOURIER_GROUPS, FOURIER_GROUP_DIM).astype(jnp.float32)
    y = jnp.fft.fft2(f, axes=(1, 3), norm='ortho').real
    return y.reshape(b, n, FOURIER_W).astype(pf.dtype)

def merge_branches(pg, yd, ym, yf, w_bd, w_bm, w_bf, w_o):
    g = jax.nn.sigmoid(pg.reshape(pg.shape[:-1] + (N_BRANCHES, D_MODEL)))
    merged = g[..., 0, :] * (yd @ w_bd) + g[..., 1, :] * (ym @ w_bm) + g[..., 2, :] * (yf @ w_bf)
    return merged @ w_o

def setup_inputs(seed: int = 0) -> dict:
    key = jax.random.key(seed)
    ks = jax.random.split(key, 24)

    def nrm(k, shape, s):
        return jax.random.normal(k, shape, jnp.float32) * s

    def gain(k, shape):
        return 1.0 + 0.02 * jax.random.normal(k, shape, jnp.float32)

    return {
        'x': nrm(ks[0], (BATCH, SEQ, D_MODEL), 1.0),
        'c': nrm(ks[1], (BATCH, D_MODEL), 1.0),
        'ctx': nrm(ks[2], (BATCH, CTX_LEN, D_MODEL), 1.0),
        'c_ctx': nrm(ks[3], (D_MODEL,), 1.0),
        'ada_w': nrm(ks[4], (DEPTH, D_MODEL, N_MOD * D_MODEL), 0.5 * D_MODEL ** -0.5),
        'ada_b': nrm(ks[5], (DEPTH, N_MOD * D_MODEL), 0.02),
        'norm_g': gain(ks[6], (DEPTH, 3, D_MODEL)),
        'ffn_w_in': nrm(ks[7], (DEPTH, 2, D_MODEL, 2 * D_FF), D_MODEL ** -0.5),
        'ffn_w_out': nrm(ks[8], (DEPTH, 2, D_FF, D_MODEL), D_FF ** -0.5),
        'w_in': nrm(ks[9], (DEPTH, D_MODEL, IN_WIDTH), D_MODEL ** -0.5),
        'diff_lambda': nrm(ks[10], (DEPTH, 4, DIFF_HD), 0.1),
        'diff_subln_g': gain(ks[11], (DEPTH, DIFF_VD)),
        'mla_q_norm_g': gain(ks[12], (DEPTH, MLA_Q_RANK)),
        'mla_w_uq': nrm(ks[13], (DEPTH, MLA_Q_RANK, MLA_HEADS * (MLA_NOPE + MLA_ROPE)), MLA_Q_RANK ** -0.5),
        'mla_kv_norm_g': gain(ks[14], (DEPTH, MLA_KV_RANK)),
        'mla_w_ukv': nrm(ks[15], (DEPTH, MLA_KV_RANK, MLA_HEADS * (MLA_NOPE + MLA_VD)), MLA_KV_RANK ** -0.5),
        'w_branch_diff': nrm(ks[16], (DEPTH, DIFF_V_W, D_MODEL), DIFF_V_W ** -0.5),
        'w_branch_mla': nrm(ks[17], (DEPTH, MLA_OUT_W, D_MODEL), MLA_OUT_W ** -0.5),
        'w_branch_fourier': nrm(ks[18], (DEPTH, FOURIER_W, D_MODEL), FOURIER_W ** -0.5),
        'w_out': nrm(ks[19], (DEPTH, D_MODEL, D_MODEL), D_MODEL ** -0.5),
        'final_norm_g': gain(ks[20], (D_MODEL,)),
    }

def reference(x, c, ctx, c_ctx, ada_w, ada_b, norm_g, ffn_w_in, ffn_w_out, w_in, diff_lambda,
              diff_subln_g, mla_q_norm_g, mla_w_uq, mla_kv_norm_g, mla_w_ukv, w_branch_diff,
              w_branch_mla, w_branch_fourier, w_out, final_norm_g):
    n_lat = x.shape[1]
    rows = n_lat // GRID_W
    t_row = jnp.repeat(jnp.arange(rows), GRID_W)
    t_col = jnp.tile(jnp.arange(GRID_W), rows)
    cos_d, sin_d = axial_rope_tables(t_row, t_col, DIFF_HD)
    cos_m, sin_m = axial_rope_tables(t_row, t_col, MLA_ROPE)

    for l in range(DEPTH):
        last = l == DEPTH - 1
        mx = jnp.split((jax.nn.silu(c) @ ada_w[l] + ada_b[l])[:, None, :], N_MOD, axis=-1)
        mc = jnp.split(jax.nn.silu(c_ctx) @ ada_w[l] + ada_b[l], N_MOD, axis=-1)

        x = x + 0.5 * mx[2] * swiglu(modulate(rms_norm(x, norm_g[l, 0]), mx[0], mx[1]),
                                     ffn_w_in[l, 0], ffn_w_out[l, 0])
        ctx = ctx + 0.5 * mc[2] * swiglu(modulate(rms_norm(ctx, norm_g[l, 0]), mc[0], mc[1]),
                                         ffn_w_in[l, 0], ffn_w_out[l, 0])

        px = split_proj(modulate(rms_norm(x, norm_g[l, 1]), mx[3], mx[4]) @ w_in[l])
        pc = split_proj(modulate(rms_norm(ctx, norm_g[l, 1]), mc[3], mc[4]) @ w_in[l])

        lam_init = 0.8 - 0.6 * math.exp(-0.3 * l)
        lam = (jnp.exp(jnp.sum(diff_lambda[l, 0] * diff_lambda[l, 1]))
               - jnp.exp(jnp.sum(diff_lambda[l, 2] * diff_lambda[l, 3])) + lam_init)
        q1x, q2x, k1x, k2x, vx = diff_qkv(px[0], px[1], px[2])
        q1x, q2x, k1x, k2x = (axial_rope(t, cos_d, sin_d) for t in (q1x, q2x, k1x, k2x))
        q1c, q2c, k1c, k2c, vc = diff_qkv(pc[0], pc[1], pc[2])
        k1 = jnp.concatenate([k1c, k1x], axis=2)
        k2 = jnp.concatenate([k2c, k2x], axis=2)
        vd = jnp.concatenate([vc, vx], axis=2)
        od_x = sweep_query_blocks(lambda a, b: diff_attend(a, b, k1, k2, vd, lam), (q1x, q2x))
        yd_x = diff_out(od_x, diff_subln_g[l], lam_init)

        qnx, qrx, knx, vmx = mla_qkv(px[3], px[4], mla_q_norm_g[l], mla_w_uq[l], mla_kv_norm_g[l], mla_w_ukv[l])
        qrx = axial_rope(qrx, cos_m, sin_m)
        krx = axial_rope(px[5], cos_m, sin_m)
        qnc, qrc, knc, vmc = mla_qkv(pc[3], pc[4], mla_q_norm_g[l], mla_w_uq[l], mla_kv_norm_g[l], mla_w_ukv[l])
        krc = pc[5]
        kn = jnp.concatenate([knc, knx], axis=2)
        kr = jnp.concatenate([krc, krx], axis=1)
        vm = jnp.concatenate([vmc, vmx], axis=2)
        om_x = sweep_query_blocks(lambda a, b: mla_attend(a, b, kn, kr, vm), (qnx, qrx))
        ym_x = merge_heads(om_x)

        yf_x = fourier_mix(px[6])

        x = x + mx[5] * merge_branches(px[7], yd_x, ym_x, yf_x, w_branch_diff[l], w_branch_mla[l],
                                       w_branch_fourier[l], w_out[l])
        x = x + 0.5 * mx[8] * swiglu(modulate(rms_norm(x, norm_g[l, 2]), mx[6], mx[7]),
                                     ffn_w_in[l, 1], ffn_w_out[l, 1])

        if not last:
            od_c = diff_attend(q1c, q2c, k1c, k2c, vc, lam)
            yd_c = diff_out(od_c, diff_subln_g[l], lam_init)
            ym_c = merge_heads(mla_attend(qnc, qrc, knc, krc, vmc))
            yf_c = fourier_mix(pc[6])
            ctx = ctx + mc[5] * merge_branches(pc[7], yd_c, ym_c, yf_c, w_branch_diff[l], w_branch_mla[l],
                                               w_branch_fourier[l], w_out[l])
            ctx = ctx + 0.5 * mc[8] * swiglu(modulate(rms_norm(ctx, norm_g[l, 2]), mc[6], mc[7]),
                                             ffn_w_in[l, 1], ffn_w_out[l, 1])

    return rms_norm(x, final_norm_g)


_drawn_inputs = setup_inputs


def setup_inputs(seed=0):
    import zlib

    import numpy as np

    out = dict(_drawn_inputs(seed))
    spreads = {}
    factors = {'norm_g': 6.937,
     'diff_lambda': 8.0,
     'diff_subln_g': 8.0,
     'mla_q_norm_g': 8.0,
     'mla_w_uq': 2.765,
     'mla_kv_norm_g': 8.0,
     'final_norm_g': 2.957}
    for name, (base, spread) in spreads.items():
        noise = np.random.default_rng([zlib.crc32(name.encode()), seed]).standard_normal(out[name].shape)
        drawn = base * np.exp(spread * noise) if base else spread * noise
        out[name] = __import__('jax').numpy.asarray(drawn.astype(out[name].dtype))
    for name, factor in factors.items():
        out[name] = (out[name] * factor).astype(out[name].dtype)
    return out
```

```python
import math
from contextlib import ExitStack, nullcontext

import concourse.bass as bass
from concourse import mybir
import numpy as np

F32 = mybir.dt.float32
F32R = mybir.dt.float32r
ACT = mybir.ActivationFunctionType
ALU = mybir.AluOpType
AX_X = mybir.AxisListType.X
ds = bass.ds

P = 128
D_MODEL, SEQ, CTX_LEN, DEPTH, GRID_W = 1024, 256, 256, 2, 64
TOK = CTX_LEN + SEQ
DC = D_MODEL // P
N_MOD = 9
D_FF = 2816
FT = D_FF // P
DIFF_HEADS, DIFF_HD = 4, 64
MLA_HEADS, MLA_NOPE, MLA_ROPE, MLA_VD = 8, 64, 32, 64
MLA_QD = MLA_NOPE + MLA_ROPE
Q_RANK, KV_RANK = 384, 256
QC, KVC = Q_RANK // P, KV_RANK // P
FG = 4
NB = 3
RMS_EPS = 1e-6
ROPE_BASE = 10000.0
IN_OFF = np.cumsum([0, 512, 512, 512, Q_RANK, KV_RANK, MLA_ROPE, 512])
LAM_INIT = [0.8 - 0.6 * math.exp(-0.3 * l) for l in range(DEPTH)]

RAW = 4
H = 1024
F_HALVES = [12, 10]
MODT = N_MOD * DC
CTX, LAT = slice(0, CTX_LEN), slice(CTX_LEN, TOK)
S_X, S_C = 0, 1
FREE = 2


WALLS = 8
ROPES = 9
PARTS = 11
DVE_LAM = 1 + DEPTH + 1
Y_TOTAL = DEPTH * (3 * DC + DIFF_HEADS + QC + KVC) + DC


def unit_plan():
    c = dict(u=0, q=0, f=0, a=0, g=0, d=0, f_all=0)
    marks, units = {}, []

    def mark(name, **k):
        marks[name] = dict(c, **k)

    def add(kind, n, w, job=True):
        for _ in range(n):
            units.append((kind, w))
        c["u"] += n
        c["q"] += n if job else 0

    mark("start")
    add("ada", 8, (1024, 1024), job=False)
    c["a"] += 4
    c["d"] += DC

    def ffn(l, k, with_ada):
        for part, nf in enumerate(F_HALVES):
            mark(("up", l, k, part), bodies=with_ada[part])
            nb = with_ada[part]
            for _ in range(nb):
                add("ada", 2, (1024, 1024), job=False)
                c["a"] += 1
                add("up", 2, (1024, 1024))
            add("up", nf - 2 * nb, (1024, 1024))
            c["f"] += nf
            mark(("down", l, k, part))
            add(f"dn{part}", DC, (nf * 64, nf * 64))
            if part:
                c["d"] += DC

    for l in range(DEPTH):
        last = l == DEPTH - 1
        ffn(l, 0, [6, 5] if not last else [6, 3])
        mark(("qkv", l))
        if l == 0:
            add("ada", 2, (1024, 1024), job=False)
            c["a"] += 1
        add("proj", 6, (1024, 1024))
        mark(("latent", l))
        add("proj", 2, (1024, 1024))
        add("kr", 1, (1024, 768))
        mark(("mla", l))
        add("kvv", 2, (256, 256))
        for _ in range(4):
            add("uq", 1, (QC * MLA_QD, QC * MLA_QD))
            add("kvk", 1, (256, 256))
        mark(("four", l))
        add("proj", 2, (1024, 1024))
        mark(("merge", l))
        add("merge", DC * NB, (1024, 512))
        c["g"] += DC * NB
        mark(("wout", l))
        add("wout", DC, (512, 512))
        c["d"] += DC
        ffn(l, 1, [6, 5] if not last else [0, 0])
    mark("end")
    assert c["a"] == DEPTH * MODT // 4, c
    return marks, units


MARKS, UNITS = unit_plan()
KINDS = ["ada", "up", "dn0", "dn1", "proj", "kr", "kvv", "uq", "kvk", "merge", "wout"]


def build(nc, A):
    M = MARKS
    with ExitStack() as ctx:
        def sb(name, shape, dt=F32):
            return ctx.enter_context(nc.sbuf_tensor(name, shape, dt))

        def sem(name):
            return ctx.enter_context(nc.semaphore(name))

        x = sb("x_res", [P, DC, TOK])
        xnh = sb("xn_hi", [P, DC, TOK], F32R)
        xnl = sb("xn_lo", [P, DC, TOK], F32R)
        raw = sb("w_raw", [P, RAW, 2, H])
        wh = sb("w_hi", [P, 2, 2, H], F32R)
        wl = sb("w_lo", [P, 2, 2, H], F32R)
        R = sb("split_scratch", [P, 12288], F32R)
        S = sb("scratch", [P, 8192])
        mods = sb("mods", [P, 2, DEPTH * MODT])
        adab = sb("ada_bias", [P, DEPTH * MODT])
        cz = sb("c_split", [P, DC, 76], F32R)
        ident = sb("ident", [P, P])
        ones = sb("ones", [P, 2])
        eps = sb("eps", [P, 1])
        ada_rows = sb("ada_rows", [72, 256])
        ada_sum = sb("ada_sum", [P, 8])
        rope_d = sb("rope_d", [P, 2, SEQ])
        rope_m = sb("rope_m", [P, 2, SEQ])
        kr = sb("k_rope", [MLA_QD, TOK])
        rope_t = sb("rope_tmp", [P, SEQ])
        gains = sb("gains", [P, DEPTH * 3 * DC])
        gfin = sb("gain_final", [P, DC])
        gsub = sb("gain_sub", [P, DEPTH])
        gq = sb("gain_q", [P, DEPTH * QC])
        gkv = sb("gain_kv", [P, DEPTH * KVC])
        vec = sb("vectors", [P, DC, 2])
        vsil = sb("vectors_silu", [P, DC, 2])
        amul = sb("norm_scale", [P, 2, DC])
        ghalf = sb("gate_half", [P, 2, DC])
        sd = sb("norm_std", [P, 16])
        rs = sb("norm_rstd", [P, 16])
        nlam = sb("neg_lambda", [P, DEPTH])
        lamp = sb("lambda_parts", [P, DEPTH, 2])
        mx = sb("score_max", [P, 2, 2])
        nm = sb("score_negmax", [P, 2, 2])
        sm = sb("prob_sum", [P, 2, 2])
        rr = sb("prob_rsum", [P, 2, 2])

        ps = ctx.enter_context(nc.psum_tensor("ps", [P, 8, 512], F32))
        B_ADA, B_T, B_ST, B_RB = 4, 5, 6, 7
        B_TR, B_O, B_S = 6, 7, 4

        SA, SB, SC, SD = (S[:, 2048 * k:2048 * (k + 1)] for k in range(4))

        def v(ap, pat, **k):
            return ap.rearrange(pat, **k)

        acc = SB[:, 1024:1536]
        sq = v(SB[:, 0:1024], "p (b n) -> p b n", b=2)
        nt = v(SA[:, 0:1024], "p (b n) -> p b n", b=2)
        ny = v(SA[:, 1024:2048], "p (b n) -> p b n", b=2)
        nt_d = v(SD[:, 0:1024], "p (b n) -> p b n", b=2)
        ny_d = v(SD[:, 1024:2048], "p (b n) -> p b n", b=2)
        sil = v(SC[:, 0:1024], "p (b n) -> p b n", b=2)
        ht = v(SC[:, 1024:2048], "p (b n) -> p b n", b=2)
        hh = v(R[:, 0:6144], "p (f n) -> p f n", f=12)
        hl = v(R[:, 6144:12288], "p (f n) -> p f n", f=12)
        Qf = v(SA, "p (h n) -> p h n", h=4)
        Vt = v(SB, "p (t n) -> p t n", t=4)
        Kf = v(SC, "p (h n) -> p h n", h=4)
        Pd = v(SC, "p (b m n) -> p b m n", b=2, m=2)
        WT = v(SD, "p (b k n) -> p b k n", b=2, k=4)
        CQ = v(S[:, 4096 + 1024:4096 + 1024 + 2560], "p (c n) -> p c n", c=5)
        Pm = v(SC[:, 0:1024], "p (b n) -> p b n", b=2)
        QF = v(SC[:, 1024:2048], "p (b n) -> p b n", b=2)
        YM = v(SA, "p (c n) -> p c n", c=4)
        YDh, YDl = (v(R[:, a:a + 2048], "p (c n) -> p c n", c=4) for a in (0, 2048))
        YMh, YMl = (v(R[:, a:a + 2048], "p (c n) -> p c n", c=4) for a in (4096, 6144))
        YFh, YFl = (v(R[:, a:a + 2048], "p (c n) -> p c n", c=4) for a in (8192, 10240))
        Kh, Kl = YMh, YMl
        QM = v(R[:, 8192:12288], "p (b m z n) -> p b m z n", b=2, m=2, z=2)
        CNh, CNl = (v(R[:, a:a + 1536], "p (c n) -> p c n", c=3) for a in (4096, 5632))
        CKh, CKl = (v(R[:, a:a + 1024], "p (c n) -> p c n", c=2) for a in (7168, 8192))
        MKh, MKl = R[:, 9216:9728], R[:, 9728:10240]
        MQ = v(R[:, 10240:12288], "p (b z n) -> p b z n", b=2, z=2)
        Ff = v(SC, "p (g n) -> p g n", g=4)
        AB = v(SB[:, 0:1024], "p (b t n) -> p b t n", b=2, t=2)
        DFT_D = SD[:, 0:256]
        DFT_C = v(SD[:, 256:768], "p (t n) -> p t n", t=2)
        DFT_S = v(SD[:, 768:1280], "p (t n) -> p t n", t=2)
        ROT_D = SD[:, 1280:1408]
        ROT_M = sb("rope_rot_m", [MLA_QD, MLA_QD])
        MG = v(S[:, 4096:8192], "p (m n) -> p m n", m=DC)
        sig = v(SA[:, 0:1024], "p (b n) -> p b n", b=2)
        prod = v(SA[:, 1024:2048], "p (b n) -> p b n", b=2)
        out_y = v(SC, "p (m n) -> p m n", m=DC)

        raw_loaded = [sem(f"raw_loaded{k}") for k in range(RAW)]
        c_loaded = sem("c_loaded")
        consts_loaded = sem("consts_loaded")
        tables_loaded = sem("tables_loaded")
        out_stored = sem("out_stored")
        hi_ready = sem("hi_ready")
        split_ready = sem("split_ready")
        half_used = sem("half_used")
        psum_free = sem("psum_free")
        silu_ready = sem("silu_ready")
        hhi_ready = sem("hhi_ready")
        h_ready = sem("h_ready")
        sq_ready = sem("sq_ready")
        acc_ready = sem("acc_ready")
        ada_staged = sem("ada_staged")
        ada_turned = sem("ada_turned")
        ada_summed = sem("ada_summed")
        mods_ready = sem("mods_ready")
        setup_ready = sem("setup_ready")
        stat_done = sem("stat_done")
        std_ready = sem("std_ready")
        rstd_ready = sem("rstd_ready")
        rb_ready = sem("rb_ready")
        rb_used = sem("rb_used")
        y_ready = sem("y_ready")
        yhi_ready = sem("yhi_ready")
        ylo_ready = sem("ylo_ready")
        sig_ready = sem("sig_ready")
        prod_ready = sem("prod_ready")
        merge_ready = sem("merge_ready")
        rot_done = sem("rot_done")
        rot_used = sem("rot_used")
        part_hi = sem("part_hi")
        part_lo = sem("part_lo")
        qhi_ready = sem("qhi_ready")
        q_ready = sem("q_ready")
        qk_done = sem("qk_done")
        negmax_ready = sem("negmax_ready")
        exp_done = sem("exp_done")
        w_ready = sem("w_ready")
        tr_done = sem("tr_done")
        wt_ready = sem("wt_ready")
        pv_done = sem("pv_done")
        o_ready = sem("o_ready")
        ab_done = sem("ab_done")
        ab_ready = sem("ab_ready")
        yf_done = sem("yf_done")
        yf_hi = sem("yf_hi")
        yf_ready = sem("yf_ready")
        nt_ready = sem("nt_ready")
        qf_ready = sem("qf_ready")
        mpair_ready = sem("mpair_ready")
        dve_chain = sem("dve_chain")
        act_chain = sem("act_chain")
        pool_chain = sem("pool_chain")
        phase_end = {e: sem(f"phase_end_{e}") for e in ("pe", "act", "dve", "pool")}

        block = ctx.enter_context(nc.Block())

        def streams(both):
            return [(CTX, S_C), (LAT, S_X)] if both else [(LAT, S_X)]

        def width(both):
            return slice(0, TOK) if both else LAT

        def phase_wall(eng, me, walls):
            eng.drain().then_inc(phase_end[me], 1)
            walls[0] += 1
            for other in phase_end:
                if other != me:
                    eng.wait_ge(phase_end[other], walls[0])

        def ahead(u, per, n):
            ws = [UNITS[u + per * i][1] for i in range(n) if u + per * i < len(UNITS)]
            return max(w[0] for w in ws), max(w[1] for w in ws)

        def up_runs(l, k, part):
            m = M[("up", l, k, part)]
            u, q, f, a, n = m["u"], m["q"], m["f"], m["a"], m["bodies"]
            out = []
            if n:
                out.append((u, q, f, a, 2, n))
                u, q, f = u + 4 * n, q + 2 * n, f + 2 * n
            left = F_HALVES[part] - 2 * n
            if left // 4:
                out.append((u, q, f, None, 4, left // 4))
                u, q, f = u + left // 4 * 4, q + left // 4 * 4, f + left // 4 * 4
            if left % 4:
                out.append((u, q, f, None, left % 4, 1))
            return out

        def loop(eng, n):
            return eng.Fori(0, n) if n > 1 else nullcontext(0)

        def item_list(l, heads):
            items, pairs = [], []
            for h in range(heads):
                for cols, nk in [(LAT, TOK)] + ([(CTX, CTX_LEN)] if l < DEPTH - 1 else []):
                    for t in range(2):
                        items.append((h, len(pairs), t, cols.start + t * P, nk))
                    pairs.append((h, cols, nk))
            return items, pairs

        def head_squares(h):
            return SC[:, 512 * h:512 * (h + 1)]

        @block.sync
        def _(sp):
            at = {k: 0 for k in KINDS}
            W = (1024, 1024)

            def load_units(u0, body, n=1):
                per = {k: sum(b[0] == k for b in body) for k, _ in body}
                assert n == 1 or (len(body) % RAW == 0 and u0 >= RAW)
                with loop(sp, n) as i:
                    seen = dict.fromkeys(per, 0)
                    for j, (kind, w) in enumerate(body):
                        u, nth = u0 + j, at[kind] + seen[kind]
                        seen[kind] += 1
                        slot = u % RAW
                        if u >= RAW:
                            sp.wait_ge(split_ready, 2 * (u - RAW) + 2 + i * (2 * len(body)))
                        src = A[kind][nth] if n == 1 else \
                            A[kind][ds(i * per[kind] + nth, 1)].rearrange("a p n -> p (a n)")
                        if w[0] == w[1]:
                            dst = raw[:, slot, :, 0:w[0]]
                            src = src.rearrange("p (h n) -> p h n", h=2)
                        else:
                            dst = raw[:, slot].rearrange("p h n -> p (h n)")[:, 0:w[0] + w[1]]
                        sp.dma_start(dst, src).then_inc(raw_loaded[slot], 16)
                for k in per:
                    at[k] += per[k] * n

            sp.dma_start(vec[:], A["vec"]).then_inc(c_loaded, 16)
            sp.dma_start(adab[:], A["ada_b"]).then_inc(c_loaded, 16)
            load_units(0, [("ada", W)] * 4)
            for dst, src in ((x[:, :, CTX], A["ctxT"]), (x[:, :, LAT], A["xT"]), (gains[:], A["norm_g"]),
                             (gfin[:], A["final_g"]), (gsub[:], A["sub_g"]), (gq[:], A["q_g"]),
                             (gkv[:], A["kv_g"]), (rope_d[:], A["rope_d"]), (rope_m[:], A["rope_m"]),
                             (ROT_M[:], A["rot_m"]), (SD[:, 0:512], A["lam"])):
                sp.dma_start(dst, src).then_inc(consts_loaded, 16)
            load_units(4, [("ada", W)] * 4)

            def load_ffn(l, k):
                for part, nf in enumerate(F_HALVES):
                    for u, _, _, a, tiles, n in up_runs(l, k, part):
                        load_units(u, ([("ada", W)] * 2 if a is not None else []) + [("up", W)] * tiles, n)
                    load_units(M[("down", l, k, part)]["u"], [(f"dn{part}", (nf * 64,) * 2)] * 4, DC // 4)

            for l in range(DEPTH):
                load_ffn(l, 0)
                load_units(M[("qkv", l)]["u"], ([("ada", W)] * 2 if l == 0 else []) + [("proj", W)] * 6)
                for e in phase_end:
                    sp.wait_ge(phase_end[e], WALLS * l + 1)
                sp.dma_start(ROT_D, A["rot_d"]).then_inc(tables_loaded, 16)
                load_units(M[("latent", l)]["u"], [("proj", W)] * 2 + [("kr", (1024, 768))]
                           + [("kvv", (256, 256))] * 2 + [("uq", (QC * MLA_QD,) * 2), ("kvk", (256, 256))] * 4)
                load_units(M[("four", l)]["u"], [("proj", W)] * 2)
                for e in phase_end:
                    sp.wait_ge(phase_end[e], WALLS * l + 6)
                sp.dma_start(SD[:, 0:1280], A["dft"]).then_inc(tables_loaded, 16)
                load_units(M[("merge", l)]["u"], [("merge", (1024, 512))] * 12, 2)
                load_units(M[("wout", l)]["u"], [("wout", (512, 512))] * 4, DC // 4)
                load_ffn(l, 1)
            sp.wait_ge(y_ready, Y_TOTAL)
            sp.dma_start(A["out"], out_y).then_inc(out_stored, 16)
            sp.wait_ge(out_stored, 16)

        @block.tensor
        def _(pe):
            walls, done = [0], dict(norm=0, group=0, chunk=0, item=0, pair=0, rot=0, part=0, head=0,
                                    qf=0, four=0, wout=0)

            def half(u, h, i=0, per=0):
                pe.wait_ge(split_ready, 2 * u + h + 1 + i * (2 * per))

            def pair_free(q, i=0, per=0):
                pe.wait_ge(psum_free, FREE + q - 1 + i * per)
                return 2 * (q % 2)

            def product(out, wtile, hi, lo, first, last, m=P):
                w_hi, w_lo = wtile
                nc.tensor.matmul(out, w_hi, hi, start=first, stop=False)
                nc.tensor.matmul(out, w_lo, hi, start=False, stop=False)
                return nc.tensor.matmul(out, w_hi, lo, start=False, stop=last)

            def wtile(u, h, k, n=P):
                cols = slice(k * n, (k + 1) * n)
                return wh[:, u % 2, h, cols], wl[:, u % 2, h, cols]

            def feature_tile(u, h, out, k0, nk, first, last, hi, lo, cols, n=P):
                for kk in range(nk):
                    ins = product(out, wtile(u, h, kk, n), hi[:, k0 + kk, cols], lo[:, k0 + kk, cols],
                                  first and kk == 0, last and kk == nk - 1)
                return ins

            def ada_unit(u, un, a, i=0, per=0):
                if un == 0:
                    pe.wait_ge(ada_staged, a + i)
                for h in range(2):
                    half(u, h, i, per)
                    for kk in range(4):
                        c = cz[:, 4 * h + kk, 4:76] if un == 0 else cz[:, 4 * h + kk, 0:72]
                        cols = slice(256 * kk, 256 * kk + 256)
                        nc.tensor.matmul(ps[0:72, B_ADA, 0:256], c, wh[:, u % 2, h, cols],
                                         start=(un == h == kk == 0), stop=False)
                        ins = nc.tensor.matmul(ps[0:72, B_ADA, 0:256], c, wl[:, u % 2, h, cols],
                                               start=False, stop=(un == 1 and h == 1 and kk == 3))
                    ins.then_inc(half_used, 1)

            def ada_turn(a, i=0):
                pe.wait_ge(ada_staged, a + 1 + i)
                pe.wait_ge(mods_ready, a + i)
                for cb in range(2):
                    ins = nc.tensor.transpose(ps[:, B_T, 72 * cb:72 * cb + 72],
                                              ada_rows[:, cb * P:(cb + 1) * P], ident[0:72, 0:72])
                ins.then_inc(ada_turned, 1)

            def norm(groups):
                k = 0
                for sums, cols, nch in groups:
                    for t in range(cols.start, cols.stop, P):
                        ins = nc.tensor.matmul(ps[:, B_ST, 2 * k:2 * k + 2], sums[:, t:t + P], ones[:],
                                               start=True, stop=True)
                        k += 1
                done["norm"] += 1
                ins.then_inc(stat_done, 1)
                pe.wait_ge(rstd_ready, done["norm"])
                k = 0
                for sums, cols, nch in groups:
                    pe.wait_ge(rb_used, FREE + done["group"] - 1)
                    bank = (B_RB, B_ADA)[done["group"] % 2]
                    for t in range(cols.start, cols.stop, P):
                        ins = nc.tensor.matmul(ps[:, bank, t:t + P], rs[:, k:k + 1].to_broadcast([P, P]),
                                               ident[:], start=True, stop=True)
                        k += 1
                    done["group"] += 1
                    ins.then_inc(rb_ready, 1)
                    done["chunk"] += nch

            def x_norm(l, k):
                m = M["start"] if (l, k) == (0, 0) else M[("down", l - 1, 1, 1) if k == 0 else
                                                          ("down", l, 0, 1) if k == 1 else ("wout", l)]
                pe.wait_ge(acc_ready, FREE + m["d"] + DC)
                norm([(acc, width(l < DEPTH - 1 or k < 2), DC)])

            def ffn(l, k):
                both = l < DEPTH - 1 or k == 0
                cols = width(both)
                for part, nf in enumerate(F_HALVES):
                    if part == 0:
                        pe.wait_ge(ylo_ready, FREE + done["chunk"])
                    for u0, q0, f0, a0, tiles, n in up_runs(l, k, part):
                        per = tiles + (2 if a0 is not None else 0)
                        with loop(pe, n) as i:
                            u = u0
                            if a0 is not None:
                                ada_unit(u, 0, a0, i, per)
                                ada_unit(u + 1, 1, a0, i, per)
                                u += 2
                            for j in range(tiles):
                                b = pair_free(q0 + j, i, tiles)
                                for h in range(2):
                                    half(u, h, i, per)
                                    feature_tile(u, h, ps[:, b + h, cols], 0, DC, True, True, xnh, xnl, cols
                                                 ).then_inc(half_used, 1)
                                u += 1
                                if a0 is not None and j == 0:
                                    ada_turn(a0, i)
                    m = M[("down", l, k, part)]
                    pe.wait_ge(h_ready, FREE + m["f"] - 1)
                    with loop(pe, DC // 4) as i:
                        for j in range(4):
                            u = m["u"] + j
                            b = pair_free(m["q"] + j, i, 4)
                            for h in range(2):
                                half(u, h, i, 4)
                                for kk in range(nf // 2):
                                    c = h * (nf // 2) + kk
                                    if c == nf - 1:
                                        pe.wait_ge(h_ready, FREE + m["f"])
                                    ins = product(ps[:, b, cols], wtile(u, h, kk), hh[:, c, cols], hl[:, c, cols],
                                                  c == 0, c == nf - 1)
                                ins.then_inc(half_used, 1)

            def proj(u, q, cols0, cols1=None, n1=P, k=DC, n=P, hi=(xnh, xnh), lo=(xnl, xnl)):
                b = pair_free(q)
                for h, cols in ((0, cols0), (1, cols1 or cols0)):
                    w = n if h == 0 or n != P else n1
                    half(u, h)
                    feature_tile(u, h, ps[0:w, b + h, cols], 0, k, True, True, hi[h], lo[h], cols, w
                                 ).then_inc(half_used, 1)

            def proj_tokens(u, q, k, hi, lo):
                b = pair_free(q)
                half(u, 0)
                half(u, 1)
                for t in range(TOK // P):
                    rows = slice(t * P, (t + 1) * P)
                    out = ps[:, b + t // 2, (t % 2) * 256:(t % 2) * 256 + 256]
                    for h in range(2):
                        for kk in range(k // 2):
                            c = h * (k // 2) + kk
                            w = slice(kk * 256, kk * 256 + 256)
                            ins = nc.tensor.matmul(out, hi[:, c, rows], wh[:, u % 2, h, w],
                                                   start=(c == 0), stop=False)
                            ins = nc.tensor.matmul(out, hi[:, c, rows], wl[:, u % 2, h, w], start=False, stop=False)
                            ins = nc.tensor.matmul(out, lo[:, c, rows], wh[:, u % 2, h, w],
                                                   start=False, stop=(c == k - 1))
                ins.then_inc(half_used, 2)

            def rotate(bank, off, table, src):
                n = src.shape[0]
                done["rot"] += 1
                nc.tensor.matmul(ps[0:n, bank, off:off + SEQ], table, src, start=True, stop=True
                                 ).then_inc(rot_done, 1)

            def transposes(a, nk, src):
                pe.wait_ge(w_ready, a + 1)
                pe.wait_ge(wt_ready, a)
                for kc in range(nk // P):
                    ins = nc.tensor.transpose(ps[:, B_TR, kc * P:(kc + 1) * P], src[:, kc * P:(kc + 1) * P], ident[:])
                ins.then_inc(tr_done, 1)

            def outputs(a, g, nk, rows, vcols):
                pe.wait_ge(wt_ready, a + 1)
                pe.wait_ge(o_ready, g)
                for kc in range(nk // P):
                    ins = nc.tensor.matmul(ps[rows, B_O, 0:256], Vt[:, kc, vcols], WT[:, g % 2, kc, :],
                                           start=(kc == 0), stop=(kc == nk // P - 1))
                ins.then_inc(pv_done, 1)

            def diff_attention(l):
                items, pairs = item_list(l, DIFF_HEADS)
                a0, g0 = done["item"], done["pair"]
                for t in range(len(items) + 2):
                    if t < len(items):
                        h, g, _, col, nk = items[t]
                        if t == 0 or items[t - 1][0] != h:
                            pe.wait_ge(q_ready, done["head"] + h + 1)
                        if a0 + t >= 2:
                            pe.wait_ge(exp_done, a0 + t - 1)
                        for m in range(2):
                            q_hi, q_lo = (QM[:, h % 2, m, z, col:col + P] for z in range(2))
                            out = ps[:, 2 * (t % 2) + m, 0:nk]
                            nc.tensor.matmul(out, q_hi, Kh[:, h, 0:nk], start=True, stop=False)
                            nc.tensor.matmul(out, q_lo, Kh[:, h, 0:nk], start=False, stop=False)
                            ins = nc.tensor.matmul(out, q_hi, Kl[:, h, 0:nk], start=False, stop=True)
                        ins.then_inc(qk_done, 1)
                    if 0 <= t - 1 < len(items):
                        transposes(a0 + t - 1, items[t - 1][4], Pd[:, (t - 1) % 2, 0])
                    if t >= 2 and items[t - 2][2] == 1:
                        h, g, _, _, nk = items[t - 2]
                        outputs(a0 + t - 2, g0 + g, nk, slice(0, P), slice(h * P, (h + 1) * P))
                done["item"] += len(items)
                done["pair"] += len(pairs)
                done["head"] += DIFF_HEADS

            def mla_units(l, i):
                m = M[("mla", l)]
                cols = width(l < DEPTH - 1)
                u, q = m["u"] + 2 + 2 * i, m["q"] + 2 + 2 * i
                proj(u, q, cols, k=QC, n=MLA_QD, hi=(CNh, CNh), lo=(CNl, CNl))
                proj(u + 1, q + 1, slice(0, TOK), k=KVC, hi=(CKh, CKh), lo=(CKl, CKl))
                done["qf"] += 1
                pe.wait_ge(qf_ready, done["qf"])
                for j in range(2):
                    rotate(2 * (q % 2) + j, 0, ROT_M[:], QF[0:MLA_QD, j, LAT])

            def mla_attention(l):
                items, pairs = item_list(l, MLA_HEADS)
                a0, g0 = done["item"], done["pair"]
                mla_units(l, 0)
                for t in range(len(items) + 2):
                    if t < len(items):
                        h, g, _, col, nk = items[t]
                        if t == 0 or items[t - 1][0] != h:
                            pe.wait_ge(q_ready, done["head"] + h + 1)
                        pe.wait_ge(exp_done, a0 + t - 1)
                        q_hi, q_lo = (MQ[0:MLA_QD, h % 2, z, col:col + P] for z in range(2))
                        out = ps[:, B_S + t % 2, 0:nk]
                        nc.tensor.matmul(out, q_hi, MKh[0:MLA_QD, 0:nk], start=True, stop=False)
                        nc.tensor.matmul(out, q_lo, MKh[0:MLA_QD, 0:nk], start=False, stop=False)
                        nc.tensor.matmul(out, q_hi, MKl[0:MLA_QD, 0:nk], start=False, stop=True).then_inc(qk_done, 1)
                        if h % 2 and items[t - 1][0] != h and h < MLA_HEADS - 1:
                            mla_units(l, h // 2 + 1)
                    if 0 <= t - 1 < len(items):
                        transposes(a0 + t - 1, items[t - 1][4], Pm[:, (t - 1) % 2])
                    if t >= 2 and items[t - 2][2] == 1:
                        h, g, _, _, nk = items[t - 2]
                        outputs(a0 + t - 2, g0 + g, nk, slice(64 * (h % 2), 64 * (h % 2) + 64),
                                slice(h * MLA_VD, (h + 1) * MLA_VD))
                done["item"] += len(items)
                done["pair"] += len(pairs)
                done["head"] += MLA_HEADS

            def fourier(l):
                m = M[("four", l)]
                both = l < DEPTH - 1
                for j in range(2):
                    proj(m["u"] + j, m["q"] + j, width(both))
                pe.wait_ge(psum_free, FREE + m["q"] + 2)
                pe.wait_ge(tables_loaded, 16 * (2 * l + 2))
                jobs = [(g, cols) for g in range(FG) for cols, _ in streams(both)]
                k0 = done["four"]
                for t in range(len(jobs) + 1):
                    if t < len(jobs):
                        g, cols = jobs[t]
                        if k0 + t >= 2:
                            pe.wait_ge(ab_ready, k0 + t - 1)
                        for tt in range(2):
                            c = cols.start + tt * P
                            ins = nc.tensor.matmul(ps[:, 4 + t % 2, tt * 256:tt * 256 + 256], Ff[:, g, c:c + P],
                                                   DFT_D, start=True, stop=True)
                        ins.then_inc(ab_done, 1)
                    if t >= 1:
                        pe.wait_ge(ab_ready, k0 + t)
                        if k0 + t - 1 >= 2:
                            pe.wait_ge(yf_ready, k0 + t - 2)
                        b = (t - 1) % 2
                        for tt in range(2):
                            nc.tensor.matmul(ps[:, 6 + b, 0:SEQ], AB[:, b, tt, 0:P], DFT_C[:, tt, :],
                                             start=(tt == 0), stop=False)
                            ins = nc.tensor.matmul(ps[:, 6 + b, 0:SEQ], AB[:, b, tt, P:2 * P], DFT_S[:, tt, :],
                                                   start=False, stop=(tt == 1))
                        ins.then_inc(yf_done, 1)
                done["four"] += len(jobs)

            pe.wait_ge(setup_ready, 1)
            pe.wait_ge(acc_ready, FREE)
            for a in range(4):
                ada_unit(2 * a, 0, a)
                ada_unit(2 * a + 1, 1, a)
                ada_turn(a)
            for l in range(DEPTH):
                both = l < DEPTH - 1
                x_norm(l, 0)
                ffn(l, 0)
                x_norm(l, 1)
                phase_wall(pe, "pe", walls)
                m = M[("qkv", l)]
                u, q = m["u"], m["q"]
                pe.wait_ge(ylo_ready, FREE + done["chunk"])
                if l == 0:
                    ada_unit(u, 0, m["a"])
                    ada_unit(u + 1, 1, m["a"])
                    ada_turn(m["a"])
                    u += 2
                for j in range(2):
                    proj(u + j, q + j, width(both))
                for j in range(2, 4):
                    proj(u + j, q + j, slice(0, TOK))
                for j in range(4, 6):
                    proj_tokens(u + j, q + j, DC, xnh, xnl)
                pe.wait_ge(psum_free, FREE + q + 4)
                pe.wait_ge(tables_loaded, 16 * (2 * l + 1))
                pe.wait_ge(mods_ready, m["a"] + (l == 0))
                for c in range(8):
                    if c >= 2:
                        pe.wait_ge(rot_used, ROPES * l + c - 1)
                    rotate(4 + c % 2, 0, ROT_D, (Qf if c < 4 else Kf)[:, c % 4, LAT])
                phase_wall(pe, "pe", walls)
                diff_attention(l)
                phase_wall(pe, "pe", walls)
                pe.wait_ge(part_lo, PARTS * l + 5)
                norm([(head_squares(h), width(both), 1) for h in range(DIFF_HEADS)])
                phase_wall(pe, "pe", walls)
                m = M[("latent", l)]
                u, q = m["u"], m["q"]
                proj(u, q, width(both))
                proj(u + 1, q + 1, width(both), slice(0, TOK))
                proj(u + 2, q + 2, slice(0, TOK), n1=MLA_QD)
                pe.wait_ge(psum_free, FREE + q + 3)
                rotate(B_T, 0, ROT_M[:], kr[:, LAT])
                pe.wait_ge(part_lo, PARTS * l + 6)
                norm([(SB[:, 0:512], width(both), QC), (SB[:, 512:1024], slice(0, TOK), KVC)])
                phase_wall(pe, "pe", walls)
                pe.wait_ge(ylo_ready, FREE + done["chunk"])
                m = M[("mla", l)]
                for j in range(2):
                    proj_tokens(m["u"] + j, m["q"] + j, KVC, CKh, CKl)
                mla_attention(l)
                phase_wall(pe, "pe", walls)
                fourier(l)
                phase_wall(pe, "pe", walls)
                m = M[("merge", l)]
                cols = width(both)
                ys = ((YDh, YDl), (YMh, YMl), (YFh, YFl))
                with loop(pe, 2) as i:
                    for j in range(12):
                        u, (yh, yl) = m["u"] + j, ys[j % NB]
                        b = pair_free(m["q"] + j, i, 12)
                        half(u, 0, i, 12)
                        feature_tile(u, 0, ps[:, b, cols], 0, DC, True, True, xnh, xnl, cols).then_inc(half_used, 1)
                        half(u, 1, i, 12)
                        feature_tile(u, 1, ps[:, b + 1, cols], 0, 4, True, True, yh, yl, cols).then_inc(half_used, 1)
                phase_wall(pe, "pe", walls)
                m = M[("wout", l)]
                done["chunk"] += DC
                pe.wait_ge(ylo_ready, FREE + done["chunk"])
                with loop(pe, DC // 4) as i:
                    for j in range(4):
                        u = m["u"] + j
                        b = pair_free(m["q"] + j, i, 4)
                        for h in range(2):
                            half(u, h, i, 4)
                            feature_tile(u, h, ps[:, b, cols], 4 * h, 4, h == 0, h == 1, xnh, xnl, cols
                                         ).then_inc(half_used, 1)
                x_norm(l, 2)
                ffn(l, 1)
            pe.wait_ge(acc_ready, FREE + M["end"]["d"])
            norm([(acc, LAT, DC)])

        @block.scalar
        def _(act):
            walls, done = [0], dict(norm=0, y=0, item=0, pair=0, four=0, chain=0)

            def link(ins):
                done["chain"] += 1
                ins.then_inc(act_chain, 1)
                act.wait_ge(act_chain, done["chain"])

            def round_unit(u, i=0, per=0, n=1):
                if u >= len(UNITS):
                    return
                w = ahead(u, per, n)
                act.wait_ge(raw_loaded[u % RAW], 16 * (u // RAW + 1) + i * (16 * per // RAW))
                for h in range(2):
                    if 2 * u + h >= 4:
                        act.wait_ge(half_used, 2 * u + h - 3 + i * (2 * per))
                    nc.scalar.copy(wh[:, u % 2, h, 0:w[h]], raw[:, u % RAW, h, 0:w[h]]).then_inc(hi_ready, 1)

            def used(u, h, i=0, per=0):
                act.wait_ge(half_used, 2 * u + h + 1 + i * (2 * per))

            def ada_stage(u, a, i=0, per=0):
                used(u, 1, i, per)
                act.wait_ge(ada_turned, a + i)
                nc.scalar.copy(ada_rows[:], ps[0:72, B_ADA, 0:256]).then_inc(ada_staged, 1)

            def square(d, cols, b, m, i=0):
                act.wait_ge(acc_ready, FREE + d - 1 + i)
                nc.scalar.activation(sq[:, b, cols], x[:, m, cols], ACT.Square).then_inc(sq_ready, 1)

            def norm(groups, chunks, tmp=None):
                done["norm"] += 1
                act.wait_ge(stat_done, done["norm"])
                act.wait_ge(rstd_ready, done["norm"] - 1)
                k = 0
                for n, (cols, dim) in enumerate(groups):
                    nt_ = (cols.stop - cols.start) // P
                    ins = nc.scalar.activation(sd[:, k:k + nt_], ps[:, B_ST, 2 * k:2 * (k + nt_):2], ACT.Sqrt,
                                               bias=eps[:], scale=1.0 / dim)
                    k += nt_
                ins.then_inc(std_ready, 1)
                if callable(chunks):
                    with act.Fori(0, DC // 2) as i:
                        for j in range(2):
                            round_chunk(*chunks(i * 2 + j, j), i * 2 + j, ny)
                    done["y"] += DC
                else:
                    for b, dst, cols in chunks:
                        round_chunk(b, dst, cols, 0, tmp)
                        done["y"] += 1

            def round_chunk(b, dst, cols, c, y):
                act.wait_ge(y_ready, done["y"] + 1 + c)
                nc.scalar.copy(dst[:, cols], y[:, b, cols]).then_inc(yhi_ready, 1)

            def x_norm(l, k):
                both = l < DEPTH - 1 or k < 2
                cols = width(both)
                phase = ("qkv", l) if k == 1 else ("up", l, k // 2, 0)
                act.wait_ge(half_used, 2 * M[phase]["u"])
                norm([(cols, D_MODEL)], lambda c, j: (j, xnh[:, ds(c, 1), :].rearrange("p a n -> p (a n)"), cols))

            def ffn(l, k):
                both = l < DEPTH - 1 or k == 0
                cols = width(both)
                for part, nf in enumerate(F_HALVES):
                    for u0, q0, f0, a0, tiles, n in up_runs(l, k, part):
                        per = tiles + (2 if a0 is not None else 0)
                        fl0 = f0 - M[("up", l, k, part)]["f"]
                        with loop(act, n) as i:
                            u = u0
                            if a0 is not None:
                                round_unit(u + 2, i, per, n)
                                round_unit(u + 3, i, per, n)
                                ada_stage(u + 1, a0, i, per)
                                u += 2
                            for j in range(tiles):
                                q, f, b = q0 + j, f0 + j, (f0 + j) % 2
                                round_unit(u + 2, i, per, n)
                                used(u, 0, i, per)
                                act.wait_ge(psum_free, FREE + q - 1 + i * tiles)
                                nc.scalar.activation(sil[:, b, cols], ps[:, 2 * (q % 2), cols], ACT.Silu
                                                     ).then_inc(silu_ready, 1)
                                act.wait_ge(psum_free, FREE + q + 1 + i * tiles)
                                nc.scalar.copy(tile(hh, i * tiles + fl0 + j)[:, cols], ht[:, b, cols]
                                               ).then_inc(hhi_ready, 1)
                                u += 1
                    m = M[("down", l, k, part)]
                    down(m, cols, part == 1)

            def tile(t, c):
                return t[:, c, :] if isinstance(c, int) else t[:, ds(c, 1), :].rearrange("p a n -> p (a n)")

            def down(m, cols, final):
                end = m["u"] + DC >= len(UNITS)
                for first, n in ([(0, 1), (4, 1)] if end else [(0, DC // 4)]):
                    with loop(act, n) as i:
                        for j in range(first, first + 4):
                            u, q, d = m["u"] + j, m["q"] + j, m["d"] + j
                            round_unit(u + 2, i, 4, n)
                            if final:
                                act.wait_ge(psum_free, FREE + q + 1 + i * 4)
                                act.wait_ge(acc_ready, FREE + d - 1 + i * 4)
                                nc.scalar.activation(sq[:, j % 2, cols], tile(x, i * 4 + j)[:, cols], ACT.Square
                                                     ).then_inc(sq_ready, 1)

            def scores_exp(a, banks, dst, scale, nk):
                act.wait_ge(negmax_ready, a + 1)
                if a >= 2:
                    act.wait_ge(tr_done, a - 1)
                for m, bank in enumerate(banks):
                    ins = nc.scalar.activation(dst[m][:, 0:nk], ps[:, bank, 0:nk], ACT.Exp, bias=nm[:, a % 2, m:m + 1],
                                               scale=scale, accum_out=sm[:, a % 2, m:m + 1])
                ins.then_inc(exp_done, 1)

            def copy_transposed(a, g, t, nk):
                act.wait_ge(tr_done, a + 1)
                if g >= 2:
                    act.wait_ge(pv_done, g - 1)
                nc.scalar.copy(WT[:, g % 2, 0:nk // P, t * P:(t + 1) * P],
                               ps[:, B_TR, 0:nk].rearrange("p (k n) -> p k n", n=P)).then_inc(wt_ready, 1)

            def diff_q(l, h):
                cols = width(l < DEPTH - 1)
                if h >= 2:
                    act.wait_ge(qk_done, done["item"] + (h - 1) * len(item_list(l, 1)[0]))
                nc.scalar.copy(QM[0:64, h % 2, 0, 0, cols], Qf[0:64, h, cols])
                nc.scalar.copy(QM[64:P, h % 2, 1, 0, cols], Qf[64:P, h, cols]).then_inc(qhi_ready, 1)

            def diff_attention(l):
                items, pairs = item_list(l, DIFF_HEADS)
                a0, g0 = done["item"], done["pair"]
                diff_q(l, 0)
                for t in range(len(items) + 1):
                    if t < len(items):
                        h, g, _, col, nk = items[t]
                        scores_exp(a0 + t, (2 * (t % 2), 2 * (t % 2) + 1), [Pd[:, t % 2, m] for m in range(2)],
                                   DIFF_HD ** -0.5, nk)
                        if (t == 0 or items[t - 1][0] != h) and h + 1 < DIFF_HEADS:
                            diff_q(l, h + 1)
                    if t >= 1:
                        h, g, tq, _, nk = items[t - 1]
                        copy_transposed(a0 + t - 1, g0 + g, tq, nk)
                done["item"] += len(items)
                done["pair"] += len(pairs)

            def mla_qk(l, h):
                m = M[("mla", l)]
                cols = width(l < DEPTH - 1)
                i, j = h // 2, h % 2
                uk, qk = m["u"] + 3 + 2 * i, m["q"] + 3 + 2 * i
                act.wait_ge(mpair_ready, 4 * l + i + 1)
                act.wait_ge(qk_done, done["item"] + h * len(item_list(l, 1)[0]))
                nc.scalar.copy(MQ[0:MLA_QD, j, 0, cols], QF[0:MLA_QD, j, cols])
                used(uk, 1)
                nc.scalar.copy(MKh[0:64, :], ps[0:64, 2 * (qk % 2) + j, :]).then_inc(qhi_ready, 1)

            def mla_attention(l):
                items, pairs = item_list(l, MLA_HEADS)
                a0, g0 = done["item"], done["pair"]
                m = M[("mla", l)]
                for j in range(2):
                    round_unit(m["u"] + 2 + 2 + j)
                for t in range(len(items) + 1):
                    if t < len(items):
                        h, g, _, col, nk = items[t]
                        if t == 0 or items[t - 1][0] != h:
                            mla_qk(l, h)
                        scores_exp(a0 + t, (B_S + t % 2,), [Pm[:, t % 2]], MLA_QD ** -0.5, nk)
                        if h % 2 and items[t - 1][0] != h and h < MLA_HEADS - 1:
                            for j in range(2):
                                round_unit(m["u"] + 2 + 2 * (h // 2 + 1) + 2 + j)
                    if t >= 1:
                        h, g, tq, _, nk = items[t - 1]
                        copy_transposed(a0 + t - 1, g0 + g, tq, nk)
                done["item"] += len(items)
                done["pair"] += len(pairs)

            act.wait_ge(c_loaded, 32)
            link(nc.scalar.activation(vsil[:], vec[:], ACT.Silu))
            act.wait_ge(dve_chain, 1)
            link(nc.scalar.copy(cz[:, :, 4:8:2], vsil[:]))
            round_unit(0)
            round_unit(1)
            for a in range(4):
                round_unit(2 * a + 2)
                round_unit(2 * a + 3)
                ada_stage(2 * a + 1, a)
            act.wait_ge(consts_loaded, 16 * 11)
            act.wait_ge(dve_chain, DVE_LAM)
            nc.scalar.activation(lamp[:], lamp[:], ACT.Exp).then_inc(act_chain, 1)
            done["chain"] += 1
            for c in range(DC):
                act.wait_ge(acc_ready, FREE + c - 1)
                nc.scalar.activation(sq[:, c % 2, :], x[:, c, :], ACT.Square).then_inc(sq_ready, 1)

            for l in range(DEPTH):
                both = l < DEPTH - 1
                cols = width(both)
                x_norm(l, 0)
                ffn(l, 0)
                x_norm(l, 1)
                phase_wall(act, "act", walls)
                m = M[("qkv", l)]
                u = m["u"]
                if l == 0:
                    round_unit(u + 2)
                    round_unit(u + 3)
                    ada_stage(u + 1, m["a"])
                    u += 2
                for j in range(6):
                    round_unit(u + 2 + j)
                for c in range(4):
                    act.wait_ge(rot_used, ROPES * l + 5 + c)
                    nc.scalar.copy(Kh[:, c, :], Kf[:, c, :]).then_inc(part_hi, 1)
                phase_wall(act, "act", walls)
                diff_attention(l)
                phase_wall(act, "act", walls)
                norm([(cols, 2 * DIFF_HD)] * DIFF_HEADS,
                     [(h % 2, YDh[:, h, :], cols) for h in range(DIFF_HEADS)], ny_d)
                phase_wall(act, "act", walls)
                u = M[("latent", l)]["u"]
                for j in range(3):
                    round_unit(u + 2 + j)
                norm([(cols, Q_RANK), (slice(0, TOK), KV_RANK)],
                     [(c % 2, CNh[:, c, :], cols) for c in range(QC)]
                     + [((QC + c) % 2, CKh[:, c, :], slice(0, TOK)) for c in range(KVC)], ny)
                phase_wall(act, "act", walls)
                nc.scalar.copy(MKh[64:MLA_QD, :], kr[64:MLA_QD, :]).then_inc(part_hi, 1)
                u = M[("mla", l)]["u"]
                for j in range(2):
                    round_unit(u + 2 + j)
                mla_attention(l)
                phase_wall(act, "act", walls)
                for c in range(4):
                    nc.scalar.copy(YMh[:, c, cols], YM[:, c, cols]).then_inc(part_hi, 1)
                u = M[("four", l)]["u"]
                for j in range(2):
                    round_unit(u + 2 + j)
                k0 = done["four"]
                jobs = [(g, sc_) for g in range(FG) for sc_, _ in streams(both)]
                for t in range(len(jobs) + 1):
                    if t < len(jobs):
                        act.wait_ge(ab_done, k0 + t + 1)
                        if k0 + t >= 2:
                            act.wait_ge(yf_done, k0 + t - 1)
                        nc.scalar.copy(AB[:, t % 2].rearrange("p t n -> p (t n)"), ps[:, 4 + t % 2, :]
                                       ).then_inc(ab_ready, 1)
                    if t >= 1:
                        g, sc_ = jobs[t - 1]
                        act.wait_ge(yf_done, k0 + t)
                        nc.scalar.copy(YFh[:, g, sc_], ps[:, 6 + (t - 1) % 2, 0:SEQ]).then_inc(yf_hi, 1)
                done["four"] += len(jobs)
                phase_wall(act, "act", walls)
                m = M[("merge", l)]
                with loop(act, 2) as i:
                    for j in range(12):
                        u, q = m["u"] + j, m["q"] + j
                        round_unit(u + 2, i, 12, 2)
                        used(u, 0, i, 12)
                        act.wait_ge(psum_free, FREE + q - 1 + i * 12)
                        nc.scalar.activation(sig[:, j % 2, cols], ps[:, 2 * (q % 2), cols], ACT.Sigmoid
                                             ).then_inc(sig_ready, 1)
                phase_wall(act, "act", walls)
                for c in range(DC):
                    nc.scalar.copy(xnh[:, c, cols], MG[:, c, cols]).then_inc(yhi_ready, 1)
                down(M[("wout", l)], cols, True)
                x_norm(l, 2)
                ffn(l, 1)
            norm([(LAT, D_MODEL)], [])

        @block.gpsimd
        def _(pool):
            walls, done = [0], dict(norm=0, chunk=0, chain=0)

            def link(ins):
                done["chain"] += 1
                ins.then_inc(pool_chain, 1)
                pool.wait_ge(pool_chain, done["chain"])

            def sum_squares(d, cols, n=DC):
                pool.wait_ge(stat_done, done["norm"])
                link(nc.gpsimd.memset(acc, 0.0))
                with pool.Fori(0, DC // 2) as i:
                    for j in range(2):
                        pool.wait_ge(sq_ready, d + j + 1 + i * 2)
                        pool.wait_ge(acc_ready, FREE + d + j + i * 2)
                        nc.gpsimd.tensor_tensor(acc[:, cols], acc[:, cols], sq[:, j, cols], ALU.add
                                                ).then_inc(acc_ready, 1)

            def lo_chunk(c, b, dst, hi, cols, src=None):
                pool.wait_ge(yhi_ready, done["chunk"] + 1 + c)
                s_ = ny[:, b, cols] if src is None else src
                nc.gpsimd.tensor_tensor(dst[:, cols], s_, hi[:, cols].bitcast(F32), ALU.subtract
                                        ).then_inc(ylo_ready, 1)

            def tile(t, c):
                return t[:, ds(c, 1), :].rearrange("p a n -> p (a n)")

            def x_norm(both):
                cols = width(both)
                done["norm"] += 1
                with pool.Fori(0, DC // 2) as i:
                    for j in range(2):
                        lo_chunk(i * 2 + j, j, tile(xnl, i * 2 + j), tile(xnh, i * 2 + j), cols)
                done["chunk"] += DC

            nc.gpsimd.memset(ones[:], 1.0).then_inc(ylo_ready, FREE)
            nc.gpsimd.memset(eps[:], RMS_EPS)
            link(nc.gpsimd.memset(ident[:], 0.0))
            nc.gpsimd.affine_select(out=ident[:], in_=ident[:], compare_op=ALU.not_equal, fill=1.0, base=0,
                                    pattern=[[-1, P]], channel_multiplier=1).then_inc(acc_ready, FREE)
            pool.wait_ge(acc_ready, FREE)
            sum_squares(0, slice(0, TOK))
            for l in range(DEPTH):
                both = l < DEPTH - 1
                cols = width(both)
                x_norm(True)
                sum_squares(M[("down", l, 0, 1)]["d"], slice(0, TOK))
                x_norm(True)
                phase_wall(pool, "pool", walls)
                phase_wall(pool, "pool", walls)
                phase_wall(pool, "pool", walls)
                done["norm"] += 1
                for h in range(DIFF_HEADS):
                    lo_chunk(0, h % 2, YDl[:, h, :], YDh[:, h, :], cols, src=ny_d[:, h % 2, cols])
                    done["chunk"] += 1
                phase_wall(pool, "pool", walls)
                done["norm"] += 1
                for c in range(QC + KVC):
                    if c < QC:
                        lo_chunk(0, c % 2, CNl[:, c, :], CNh[:, c, :], cols)
                    else:
                        lo_chunk(0, c % 2, CKl[:, c - QC, :], CKh[:, c - QC, :], slice(0, TOK))
                    done["chunk"] += 1
                phase_wall(pool, "pool", walls)
                phase_wall(pool, "pool", walls)
                phase_wall(pool, "pool", walls)
                phase_wall(pool, "pool", walls)
                for c in range(DC):
                    lo_chunk(0, 0, xnl[:, c, :], xnh[:, c, :], cols, src=MG[:, c, cols])
                    done["chunk"] += 1
                sum_squares(M[("wout", l)]["d"], cols)
                x_norm(both)
                sum_squares(M[("down", l, 1, 1)]["d"], cols)

        @block.vector
        def _(dve):
            walls, done = [0], dict(norm=0, group=0, chunk=0, item=0, pair=0, part=0, head=0, qhead=0, four=0,
                                    chain=0, rot=0, qf=0, y=0)

            def link(ins):
                done["chain"] += 1
                ins.then_inc(dve_chain, 1)
                dve.wait_ge(dve_chain, done["chain"])

            def split_unit(u, i=0, per=0, n=1):
                if u >= len(UNITS):
                    return
                w = ahead(u, per, n)
                for h in range(2):
                    dve.wait_ge(hi_ready, 2 * u + h + 1 + i * (2 * per))
                    nc.vector.tensor_tensor(wl[:, u % 2, h, 0:w[h]], raw[:, u % RAW, h, 0:w[h]],
                                            wh[:, u % 2, h, 0:w[h]].bitcast(F32), ALU.subtract
                                            ).then_inc(split_ready, 1)

            def used(u, h, i=0, per=0):
                dve.wait_ge(half_used, 2 * u + h + 1 + i * (2 * per))

            def tile(t, c):
                return t[:, c, :] if isinstance(c, int) else t[:, ds(c, 1), :].rearrange("p a n -> p (a n)")

            def ada_vectors(a, i=0):
                dve.wait_ge(ada_turned, a + 1 + i)
                dve.wait_ge(mods_ready, a + i)
                nc.vector.tensor_reduce(ada_sum[:].rearrange("p (c e) -> p c e", c=2),
                                        ps[:, B_T, 0:144].rearrange("p (c e z) -> p c e z", c=2, z=2)[:, :, 0:4, :],
                                        axis=AX_X, op=ALU.add).then_inc(ada_summed, 1)
                dve.wait_ge(ada_summed, a + 1 + i)
                t = slice(4 * a, 4 * a + 4) if isinstance(i, int) else ds(i * 4 + 4 * a, 4)
                out = mods[:, :, t].rearrange("p v (u c) -> p c u v", c=2)
                bias = adab[:, t].rearrange("p (u c) -> p c u", c=2)
                for v_ in range(2):
                    ins = nc.vector.tensor_tensor(out[:, :, :, v_],
                                                  ada_sum[:].rearrange("p (c u v) -> p c u v", c=2, u=2)[:, :, :, v_],
                                                  bias, ALU.add)
                ins.then_inc(mods_ready, 1)

            def norm(groups, tmp):
                done["norm"] += 1
                dve.wait_ge(std_ready, done["norm"])
                n = sum((cols.stop - cols.start) // P for cols, _ in groups)
                nc.vector.reciprocal(rs[:, 0:n], sd[:, 0:n]).then_inc(rstd_ready, 1)
                k = 0
                for cols, chunks in groups:
                    dve.wait_ge(rb_ready, done["group"] + 1)
                    bank = (B_RB, B_ADA)[done["group"] % 2]
                    if callable(chunks):
                        with dve.Fori(0, DC // 2) as i:
                            for j in range(2):
                                norm_chunk(j, bank, cols, i * 2 + j, tmp, *chunks(i * 2 + j))
                        done["chunk"] += DC
                        done["y"] += DC
                    else:
                        for chunk in chunks:
                            norm_chunk(k % 2, bank, cols, 0, tmp, *chunk)
                            k += 1
                            done["chunk"] += 1
                            done["y"] += 1
                    done["group"] += 1
                    dve.drain().then_inc(rb_used, 1)

            def norm_chunk(b, bank, cols, c, tmp, src, by_stream, dst=None):
                t_, y_ = tmp
                if dst is None:
                    dve.wait_ge(ylo_ready, FREE + done["chunk"] - 1 + c)
                nc.vector.tensor_tensor(t_[:, b, cols], src[:, cols], ps[:, bank, cols], ALU.mult
                                        ).then_inc(nt_ready, 1)
                dve.wait_ge(nt_ready, done["y"] + 1 + c)
                for st, scale, shift in by_stream:
                    out = y_[:, b, st] if dst is None else dst
                    if shift is None:
                        ins = nc.vector.tensor_scalar(out, t_[:, b, st], scale, None, ALU.mult)
                    else:
                        ins = nc.vector.tensor_scalar(out, t_[:, b, st], scale, shift, ALU.mult, ALU.add)
                ins.then_inc(y_ready, 1)

            def x_norm(l, k):
                both = l < DEPTH - 1 or k < 2
                t0 = l * MODT + 3 * k * DC
                dve.wait_ge(mods_ready, (t0 + 2 * DC) // 4)
                for _, s_ in streams(both):
                    link(nc.vector.tensor_scalar(amul[:, s_, :], mods[:, s_, t0 + DC:t0 + 2 * DC], 1.0, None, ALU.add))
                    link(nc.vector.tensor_tensor(amul[:, s_, :], amul[:, s_, :],
                                                 gains[:, (l * 3 + k) * DC:(l * 3 + k + 1) * DC], ALU.mult))

                def chunk(c):
                    return (tile(x, c), [(st, amul[:, s_, ds(c, 1)], mods[:, s_, ds(c + t0, 1)])
                                         for st, s_ in streams(both)])

                norm([(width(both), chunk)], (nt, ny))

            def gate(l, k, half_it, both):
                t0 = l * MODT + (3 * k + 2) * DC
                dve.wait_ge(mods_ready, (t0 + DC) // 4)
                for _, s_ in streams(both):
                    link(nc.vector.tensor_scalar(ghalf[:, s_, :], mods[:, s_, t0:t0 + DC], 0.5 if half_it else 1.0,
                                                 None, ALU.mult))

            def down(m, both):
                dve.wait_ge(psum_free, FREE + m["q"])
                end = m["u"] + DC >= len(UNITS)
                for first, n in ([(0, 1), (4, 1)] if end else [(0, DC // 4)]):
                    with loop(dve, n) as i:
                        for j in range(first, first + 4):
                            u, q = m["u"] + j, m["q"] + j
                            split_unit(u + 2, i, 4, n)
                            used(u, 1, i, 4)
                            c = i * 4 + j
                            for st, s_ in streams(both):
                                g = ghalf[:, s_, c:c + 1] if isinstance(c, int) else ghalf[:, s_, ds(c, 1)]
                                xt = tile(x, c)[:, st]
                                ins = nc.vector.scalar_tensor_tensor(out=xt, in0=ps[:, 2 * (q % 2), st], scalar=g,
                                                                     in1=xt, op0=ALU.mult, op1=ALU.add)
                            ins.then_inc(psum_free, 1)

            def ffn(l, k):
                both = l < DEPTH - 1 or k == 0
                cols = width(both)
                for part, nf in enumerate(F_HALVES):
                    for u0, q0, f0, a0, tiles, n in up_runs(l, k, part):
                        per = tiles + (2 if a0 is not None else 0)
                        fl0 = f0 - M[("up", l, k, part)]["f"]
                        with loop(dve, n) as i:
                            u = u0
                            if a0 is not None:
                                split_unit(u + 2, i, per, n)
                                split_unit(u + 3, i, per, n)
                                u += 2
                            for j in range(tiles):
                                q, f, b = q0 + j, f0 + j, (f0 + j) % 2
                                split_unit(u + 2, i, per, n)
                                dve.wait_ge(silu_ready, f + 1 + i * tiles)
                                used(u, 1, i, per)
                                dve.wait_ge(h_ready, FREE + f - 1 + i * tiles)
                                nc.vector.tensor_tensor(ht[:, b, cols], sil[:, b, cols],
                                                        ps[:, 2 * (q % 2) + 1, cols], ALU.mult).then_inc(psum_free, 1)
                                dve.wait_ge(hhi_ready, f + 1 + i * tiles)
                                fl = i * tiles + fl0 + j
                                nc.vector.tensor_tensor(tile(hl, fl)[:, cols], ht[:, b, cols],
                                                        tile(hh, fl)[:, cols].bitcast(F32), ALU.subtract
                                                        ).then_inc(h_ready, 1)
                                if a0 is not None and j == 0:
                                    ada_vectors(a0, i)
                                u += 1
                    if part == 0:
                        gate(l, 2 * k, True, both)
                    down(M[("down", l, k, part)], both)

            def evacuate(q, copies):
                for dst, src in copies[:-1]:
                    nc.vector.tensor_copy(dst, src)
                nc.vector.tensor_copy(*copies[-1]).then_inc(psum_free, 1)

            def values(u, q, col):
                used(u, 1)
                evacuate(q, [(Vt[:, 2 * b:2 * b + 2, col:col + 256],
                              ps[:, 2 * (q % 2) + b, :].rearrange("p (t n) -> p t n", t=2)) for b in range(2)])

            def rope(rows, src, rot, table, tmp, signal):
                done["rot"] += 1
                dve.wait_ge(rot_done, done["rot"])
                nc.vector.tensor_tensor(tmp, rot, table[rows, 1, :], ALU.mult)
                link(nc.vector.tensor_tensor(src, src, table[rows, 0, :], ALU.mult))
                nc.vector.tensor_tensor(src, src, tmp, ALU.add).then_inc(*signal)

            def negmax(a, banks, scale, nk):
                dve.wait_ge(qk_done, a + 1)
                n = len(banks)
                for m, bank in enumerate(banks):
                    ins = nc.vector.reduce_max(mx[:, a % 2, m:m + 1], ps[:, bank, 0:nk], AX_X)
                link(ins)
                nc.vector.tensor_scalar(nm[:, a % 2, 0:n], mx[:, a % 2, 0:n], -scale, None, ALU.mult
                                        ).then_inc(negmax_ready, 1)

            def diff_weights(a, l, t, nk):
                dve.wait_ge(exp_done, a + 1)
                b = a % 2
                link(nc.vector.reciprocal(rr[:, b, :], sm[:, b, :]))
                link(nc.vector.tensor_scalar(rr[:, b, 1:2], rr[:, b, 1:2], nlam[:, l:l + 1], None, ALU.mult))
                p0, p1 = Pd[:, t % 2, 0, 0:nk], Pd[:, t % 2, 1, 0:nk]
                link(nc.vector.tensor_scalar(p1, p1, rr[:, b, 1:2], None, ALU.mult))
                nc.vector.scalar_tensor_tensor(out=p0, in0=p0, scalar=rr[:, b, 0:1], in1=p1, op0=ALU.mult, op1=ALU.add
                                               ).then_inc(w_ready, 1)

            def mla_weights(a, t, nk):
                dve.wait_ge(exp_done, a + 1)
                b = a % 2
                link(nc.vector.reciprocal(rr[:, b, 0:1], sm[:, b, 0:1]))
                p = Pm[:, t % 2, 0:nk]
                nc.vector.tensor_scalar(p, p, rr[:, b, 0:1], None, ALU.mult).then_inc(w_ready, 1)

            def take_output(g, dst, rows):
                dve.wait_ge(pv_done, g + 1)
                nc.vector.tensor_copy(dst, ps[rows, B_O, 0:256]).then_inc(o_ready, 1)

            def diff_q(l, h):
                cols = width(l < DEPTH - 1)
                done["qhead"] += 1
                dve.wait_ge(qhi_ready, done["qhead"])
                for m, rows in enumerate((slice(0, 64), slice(64, P))):
                    ins = nc.vector.tensor_tensor(QM[rows, h % 2, m, 1, cols], Qf[rows, h, cols],
                                                  QM[rows, h % 2, m, 0, cols].bitcast(F32), ALU.subtract)
                ins.then_inc(q_ready, 1)

            def diff_attention(l):
                items, pairs = item_list(l, DIFF_HEADS)
                a0, g0 = done["item"], done["pair"]
                diff_q(l, 0)
                for t in range(len(items) + 2):
                    if t < len(items):
                        h, g, _, col, nk = items[t]
                        negmax(a0 + t, (2 * (t % 2), 2 * (t % 2) + 1), DIFF_HD ** -0.5, nk)
                        if (t == 0 or items[t - 1][0] != h) and h + 1 < DIFF_HEADS:
                            diff_q(l, h + 1)
                    if 1 <= t <= len(items):
                        diff_weights(a0 + t - 1, l, t - 1, items[t - 1][4])
                    if t >= 2 and items[t - 2][2] == 1:
                        h, g = items[t - 2][:2]
                        take_output(g0 + g, Qf[:, h, pairs[g][1]], slice(0, P))
                done["item"] += len(items)
                done["pair"] += len(pairs)

            def mla_units(l, i):
                m = M[("mla", l)]
                cols = width(l < DEPTH - 1)
                u, q = m["u"] + 2 + 2 * i, m["q"] + 2 + 2 * i
                for j in range(2):
                    split_unit(u + 2 + j)
                used(u, 1)
                for j in range(2):
                    ins = nc.vector.tensor_copy(QF[0:MLA_QD, j, cols], ps[0:MLA_QD, 2 * (q % 2) + j, cols])
                ins.then_inc(qf_ready, 1)
                done["qf"] += 1
                dve.wait_ge(qf_ready, done["qf"])
                rows = slice(64, MLA_QD)
                for j in range(2):
                    done["rot"] += 1
                    dve.wait_ge(rot_done, done["rot"])
                    rot = ps[rows, 2 * (q % 2) + j, 0:SEQ]
                    src = QF[rows, j, LAT]
                    ins = nc.vector.tensor_tensor(rope_t[rows, :], rot, rope_m[rows, 1, :], ALU.mult)
                    if j:
                        ins.then_inc(psum_free, 1)
                        dve.wait_ge(psum_free, FREE + q + 1)
                    else:
                        link(ins)
                    link(nc.vector.tensor_tensor(src, src, rope_m[rows, 0, :], ALU.mult))
                    ins = nc.vector.tensor_tensor(src, src, rope_t[rows, :], ALU.add)
                    if j:
                        ins.then_inc(mpair_ready, 1)
                    else:
                        link(ins)

            def mla_qk(l, h):
                m = M[("mla", l)]
                cols = width(l < DEPTH - 1)
                i, j = h // 2, h % 2
                qk = m["q"] + 3 + 2 * i
                done["qhead"] += 1
                dve.wait_ge(qhi_ready, done["qhead"])
                ins = nc.vector.tensor_tensor(MKl[0:64, :], ps[0:64, 2 * (qk % 2) + j, :],
                                              MKh[0:64, :].bitcast(F32), ALU.subtract)
                if j:
                    ins.then_inc(psum_free, 1)
                nc.vector.tensor_tensor(MQ[0:MLA_QD, j, 1, cols], QF[0:MLA_QD, j, cols],
                                        MQ[0:MLA_QD, j, 0, cols].bitcast(F32), ALU.subtract).then_inc(q_ready, 1)

            def mla_attention(l):
                items, pairs = item_list(l, MLA_HEADS)
                a0, g0 = done["item"], done["pair"]
                mla_units(l, 0)
                for t in range(len(items) + 2):
                    if t < len(items):
                        h, g, _, col, nk = items[t]
                        new = t == 0 or items[t - 1][0] != h
                        if new:
                            mla_qk(l, h)
                        negmax(a0 + t, (B_S + t % 2,), MLA_QD ** -0.5, nk)
                    if 1 <= t <= len(items):
                        mla_weights(a0 + t - 1, t - 1, items[t - 1][4])
                    if t < len(items) and new and h % 2 and h < MLA_HEADS - 1:
                        mla_units(l, h // 2 + 1)
                    if t >= 2 and items[t - 2][2] == 1:
                        h, g = items[t - 2][:2]
                        rows = slice(64 * (h % 2), 64 * (h % 2) + 64)
                        take_output(g0 + g, YM[rows, h // 2, pairs[g][1]], rows)
                done["item"] += len(items)
                done["pair"] += len(pairs)

            def sum_of_squares(dst, chunks, tmp):
                for n, c in enumerate(chunks):
                    o = dst if n == 0 else tmp
                    link(nc.vector.tensor_tensor(o, c, c, ALU.mult))
                    if n:
                        link(nc.vector.tensor_tensor(dst, dst, tmp, ALU.add))

            link(nc.vector.memset(cz[:].bitcast(F32), 0.0))
            nc.vector.memset(rs[:], 0.0).then_inc(psum_free, FREE)
            nc.vector.memset(sd[:], 0.0).then_inc(h_ready, FREE)
            nc.vector.memset(mx[:], 0.0).then_inc(rb_used, FREE)
            nc.vector.memset(nlam[:], 0.0).then_inc(merge_ready, FREE)
            dve.wait_ge(act_chain, 2)
            nc.vector.tensor_tensor(cz[:, :, 5:8:2], vsil[:], cz[:, :, 4:8:2].bitcast(F32), ALU.subtract
                                    ).then_inc(setup_ready, 1)
            split_unit(0)
            split_unit(1)
            dve.wait_ge(c_loaded, 32)
            for a in range(4):
                split_unit(2 * a + 2)
                split_unit(2 * a + 3)
                ada_vectors(a)
            dve.wait_ge(consts_loaded, 16 * 11)
            lam4 = SD[:, 0:512].rearrange("p (l a b d) -> p l a b d", l=DEPTH, a=2, b=2)
            lamt = SD[:, 512:768].rearrange("p (l a d) -> p l a d", l=DEPTH, a=2)
            for l in range(DEPTH):
                link(nc.vector.tensor_tensor(lamt[:, l], lam4[:, l, :, 0], lam4[:, l, :, 1], ALU.mult))
            link(nc.vector.tensor_reduce(lamp[:], lamt, axis=AX_X, op=ALU.add))
            assert done["chain"] == DVE_LAM
            dve.wait_ge(act_chain, 3)
            for l in range(DEPTH):
                link(nc.vector.tensor_tensor(nlam[:, l:l + 1], lamp[:, l, 1:2], lamp[:, l, 0:1], ALU.subtract))
                link(nc.vector.tensor_scalar(nlam[:, l:l + 1], nlam[:, l:l + 1], -LAM_INIT[l], None, ALU.add))
                link(nc.vector.tensor_scalar(gsub[:, l:l + 1], gsub[:, l:l + 1], 1.0 - LAM_INIT[l], None, ALU.mult))

            for l in range(DEPTH):
                both = l < DEPTH - 1
                cols = width(both)
                x_norm(l, 0)
                ffn(l, 0)
                x_norm(l, 1)
                phase_wall(dve, "dve", walls)
                m = M[("qkv", l)]
                u, q = m["u"], m["q"]
                if l == 0:
                    split_unit(u + 2)
                    split_unit(u + 3)
                    ada_vectors(m["a"])
                    u += 2
                for j in range(4):
                    split_unit(u + 2 + j)
                    used(u + j, 1)
                    c_, dst = (cols, Qf) if j < 2 else (slice(0, TOK), Kf)
                    evacuate(q + j, [(dst[:, 2 * (j % 2) + b, c_], ps[:, 2 * ((q + j) % 2) + b, c_]) for b in range(2)])
                for j in range(4, 6):
                    split_unit(u + 2 + j)
                    values(u + j, q + j, 256 * (j - 4))
                dve.wait_ge(psum_free, FREE + q + 6)
                for c in range(8):
                    src = (Qf if c < 4 else Kf)[:, c % 4, LAT]
                    rope(slice(0, P), src, ps[:, 4 + c % 2, 0:SEQ], rope_d, SD[:, 256 * (c % 2):256 * (c % 2) + 256],
                         (rot_used, 1))
                    if c >= 4:
                        done["part"] += 1
                        dve.wait_ge(part_hi, done["part"])
                        nc.vector.tensor_tensor(Kl[:, c - 4, :], Kf[:, c - 4, :], Kh[:, c - 4, :].bitcast(F32),
                                                ALU.subtract).then_inc(part_lo, 1)
                nc.vector.memset(QM[64:P, :, 0].bitcast(F32), 0.0)
                nc.vector.memset(QM[0:64, :, 1].bitcast(F32), 0.0)
                phase_wall(dve, "dve", walls)
                diff_attention(l)
                phase_wall(dve, "dve", walls)
                for h in range(DIFF_HEADS):
                    ins = nc.vector.tensor_tensor(head_squares(h)[:, cols], Qf[:, h, cols], Qf[:, h, cols], ALU.mult)
                ins.then_inc(part_lo, 1)
                norm([(cols, [(Qf[:, h, :], [(cols, gsub[:, l:l + 1], None)])]) for h in range(DIFF_HEADS)],
                     (nt_d, ny_d))
                phase_wall(dve, "dve", walls)
                m = M[("latent", l)]
                u, q = m["u"], m["q"]
                for j in range(3):
                    split_unit(u + 2 + j)
                    used(u + j, 1)
                    b = 2 * ((q + j) % 2)
                    c0_, c1_ = (cols if j < 2 else slice(0, TOK)), (cols if j < 1 else slice(0, TOK))
                    evacuate(q + j, [(CQ[:, 2 * j, c0_], ps[:, b, c0_]),
                                     (CQ[:, 2 * j + 1, c1_], ps[:, b + 1, c1_]) if j < 2 else
                                     (kr[:], ps[0:MLA_QD, b + 1, :])])
                dve.wait_ge(psum_free, FREE + q + 3)
                rows = slice(64, MLA_QD)
                rope(rows, kr[rows, LAT], ps[rows, B_T, 0:SEQ], rope_m, rope_t[rows, :], (rot_used, 1))
                sum_of_squares(SB[:, cols], [CQ[:, c, cols] for c in range(QC)], SB[:, 1024:1024 + cols.stop - cols.start])
                sum_of_squares(SB[:, 512:1024], [CQ[:, QC + c, :] for c in range(KVC)], SB[:, 1024:1536])
                dve.drain().then_inc(part_lo, 1)
                norm([(cols, [(CQ[:, c, :], [(cols, gq[:, l * QC + c:l * QC + c + 1], None)])
                              for c in range(QC)]),
                      (slice(0, TOK), [(CQ[:, QC + c, :], [(slice(0, TOK), gkv[:, l * KVC + c:l * KVC + c + 1], None)])
                                       for c in range(KVC)])], (nt, ny))
                phase_wall(dve, "dve", walls)
                done["part"] += 1
                dve.wait_ge(part_hi, done["part"])
                nc.vector.tensor_tensor(MKl[64:MLA_QD, :], kr[64:MLA_QD, :], MKh[64:MLA_QD, :].bitcast(F32),
                                        ALU.subtract).then_inc(part_lo, 1)
                m = M[("mla", l)]
                for j in range(2):
                    split_unit(m["u"] + 2 + j)
                    values(m["u"] + j, m["q"] + j, 256 * j)
                mla_attention(l)
                phase_wall(dve, "dve", walls)
                for c in range(4):
                    done["part"] += 1
                    dve.wait_ge(part_hi, done["part"])
                    nc.vector.tensor_tensor(YMl[:, c, cols], YM[:, c, cols], YMh[:, c, cols].bitcast(F32),
                                            ALU.subtract).then_inc(part_lo, 1)
                m = M[("four", l)]
                for j in range(2):
                    split_unit(m["u"] + 2 + j)
                    used(m["u"] + j, 1)
                    q = m["q"] + j
                    evacuate(q, [(Ff[:, 2 * j + b, cols], ps[:, 2 * (q % 2) + b, cols]) for b in range(2)])
                jobs = [(g, sc_) for g in range(FG) for sc_, _ in streams(both)]
                for t, (g, sc_) in enumerate(jobs):
                    done["four"] += 1
                    dve.wait_ge(yf_hi, done["four"])
                    nc.vector.tensor_tensor(YFl[:, g, sc_], ps[:, 6 + t % 2, 0:SEQ], YFh[:, g, sc_].bitcast(F32),
                                            ALU.subtract).then_inc(yf_ready, 1)
                phase_wall(dve, "dve", walls)
                m = M[("merge", l)]
                with loop(dve, 2) as i:
                    for j in range(12):
                        u, q, b = m["u"] + j, m["q"] + j, j % NB
                        mm = i * 4 + j // NB
                        n_add = 2 * (m["g"] // NB) + 2 * (j // NB) + i * 8
                        split_unit(u + 2, i, 12, 2)
                        dve.wait_ge(sig_ready, m["g"] + j + 1 + i * 12)
                        used(u, 1, i, 12)
                        s_, y_ = sig[:, j % 2, cols], ps[:, 2 * (q % 2) + 1, cols]
                        dst = tile(MG, mm)[:, cols]
                        if b == 0:
                            nc.vector.tensor_tensor(dst, s_, y_, ALU.mult).then_inc(psum_free, 1)
                        else:
                            dve.wait_ge(merge_ready, FREE + n_add)
                            nc.vector.tensor_tensor(prod[:, b - 1, cols], s_, y_, ALU.mult).then_inc(psum_free, 1)
                            dve.wait_ge(psum_free, FREE + q + 1 + i * 12)
                            dve.wait_ge(merge_ready, FREE + n_add + b - 1)
                            nc.vector.tensor_tensor(dst, dst, prod[:, b - 1, cols], ALU.add).then_inc(merge_ready, 1)
                phase_wall(dve, "dve", walls)
                done["chunk"] += DC
                gate(l, 1, False, both)
                down(M[("wout", l)], both)
                x_norm(l, 2)
                ffn(l, 1)
            norm([(LAT, [(x[:, c, :], [(LAT, gfin[:, c:c + 1], None)], out_y[:, c, :]) for c in range(DC)])], (nt, ny))
    return nc



def _rows(w):
    return w.reshape(-1, P, w.shape[-1]).transpose(1, 0, 2)


def _cols(v_):
    return np.ascontiguousarray(v_.reshape(-1, P).T)


def _tables():
    def rope(dim):
        nf = dim // 4
        freqs = np.power(np.float32(ROPE_BASE), -np.arange(nf, dtype=np.float32) / nf)
        t = np.arange(SEQ)
        ar = (t // GRID_W).astype(np.float32)[:, None] * freqs
        ac = (t % GRID_W).astype(np.float32)[:, None] * freqs
        ang = np.concatenate([ar, ar, ac, ac], -1).T
        return np.stack([np.cos(ang), np.sin(ang)], 1).astype(np.float32)

    def rotation(n, dim, first):
        r, q = np.zeros((n, n), np.float32), dim // 4
        for base in range(first, n, dim):
            for m in range(dim):
                if (m // q) % 2 == 0:
                    r[base + m + q, base + m] = -1.0
                else:
                    r[base + m - q, base + m] = 1.0
        return r

    rope_d = np.concatenate([rope(DIFF_HD)] * 2)
    rope_m = np.zeros((P, 2, SEQ), np.float32)
    rope_m[MLA_NOPE:MLA_QD] = rope(MLA_ROPE)
    k, n = np.arange(P), np.arange(SEQ)
    ang_d = 2 * np.pi * (np.outer(k, k) % P) / P
    ang_n = 2 * np.pi * (np.outer(n, n) % SEQ) / SEQ
    s = (SEQ * P) ** -0.5
    cn, sn = (f(ang_n).reshape(2, P, SEQ).transpose(1, 0, 2).reshape(P, 2 * SEQ) for f in (np.cos, np.sin))
    dft = np.concatenate([np.cos(ang_d) * s, np.sin(ang_d) * s, cn, -sn], 1).astype(np.float32)
    return dict(rope_d=rope_d, rope_m=rope_m, rot_d=rotation(P, DIFF_HD, 0),
                rot_m=rotation(MLA_QD, MLA_ROPE, MLA_NOPE), dft=dft)


def _pack(I):
    out = {k: [] for k in KINDS}

    def put(kind, *halves):
        out[kind].append(np.concatenate([h.reshape(P, -1) for h in halves], 1))

    for l in range(DEPTH):
        w = _rows(I["ada_w"][l])
        for c in range(0, N_MOD * D_MODEL, 256):
            put("ada", w[:, :, c:c + 256])
        for k in range(2):
            w = _rows(I["ffn_w_in"][l, k])
            for c in range(0, D_FF, P):
                put("up", w[:, :, c:c + P], w[:, :, D_FF + c:D_FF + c + P])
            w, c0 = _rows(I["ffn_w_out"][l, k]), 0
            for part, nf in enumerate(F_HALVES):
                for m in range(0, D_MODEL, P):
                    put(f"dn{part}", w[:, c0:c0 + nf, m:m + P])
                c0 += nf
        w = _rows(I["w_in"][l])
        o = [int(v_) for v_ in IN_OFF]

        def tiles(c):
            put("proj", w[:, :, c:c + P], w[:, :, c + P:c + 2 * P])

        for c in (0, 256, 512, 768):
            tiles(c)
        for c in (0, 256):
            put("proj", w[:, :, o[2] + c:o[2] + c + 256])
        for c in (0, 256):
            tiles(o[3] + c)
        put("kr", w[:, :, o[5] - P:o[5]], w[:, :, o[5] - MLA_NOPE:o[6]])
        for c in (0, 256):
            tiles(o[6] + c)
        wq = _rows(I["mla_w_uq"][l])
        wkv = _rows(I["mla_w_ukv"][l]).reshape(P, KVC, MLA_HEADS, P)
        for h in (0, 4):
            put("kvv", wkv[:, :, h:h + 4, MLA_NOPE:])
        for h in range(0, MLA_HEADS, 2):
            put("uq", *(wq[:, :, (h + j) * MLA_QD:(h + j + 1) * MLA_QD] for j in range(2)))
            put("kvk", *(wkv[:, :, h + j] for j in range(2)))
        wb = [_rows(I[n][l]) for n in ("w_branch_diff", "w_branch_mla", "w_branch_fourier")]
        wo = _rows(I["w_out"][l])
        for m in range(0, D_MODEL, P):
            for b in range(NB):
                c = o[7] + b * D_MODEL + m
                put("merge", w[:, :, c:c + P], wb[b][:, :, m:m + P])
            put("wout", wo[:, :, m:m + P])
    return {k: np.stack(v_) for k, v_ in out.items()}


def kernel(**inputs):
    import numpy as _np
    import concourse.bacc as _bacc
    from concourse.bass_utils import run_bass_kernel_spmd as _run

    I = {k: _np.asarray(v_) for k, v_ in inputs.items()}
    arrays = dict(_pack(I), **_tables())
    arrays["xT"] = I["x"][0].T.reshape(DC, P, SEQ).transpose(1, 0, 2)
    arrays["ctxT"] = I["ctx"][0].T.reshape(DC, P, CTX_LEN).transpose(1, 0, 2)
    arrays["vec"] = _np.stack([I["c"][0].reshape(DC, P), I["c_ctx"].reshape(DC, P)], -1).transpose(1, 0, 2)
    arrays["ada_b"] = _cols(I["ada_b"])
    arrays["norm_g"] = _cols(I["norm_g"])
    arrays["final_g"] = _cols(I["final_norm_g"])
    arrays["sub_g"] = _cols(I["diff_subln_g"])
    arrays["q_g"] = _cols(I["mla_q_norm_g"])
    arrays["kv_g"] = _cols(I["mla_kv_norm_g"])
    arrays["lam"] = _np.broadcast_to(I["diff_lambda"].reshape(1, -1), (P, DEPTH * 4 * DIFF_HD))
    arrays = {f"in_{k}": _np.ascontiguousarray(v_) for k, v_ in arrays.items()}

    nc = _bacc.Bacc("TRN2", target_bir_lowering=False, num_devices=1)
    A = {k[3:]: nc.dram_tensor(k, v_.shape, F32, kind="ExternalInput").ap() for k, v_ in arrays.items()}
    A["out"] = nc.dram_tensor("out", (P, DC, SEQ), F32, kind="ExternalOutput").ap()
    build(nc, A)
    r = _run(nc, [arrays], core_ids=[0])
    got = r.results[0]["out"]
    return got.transpose(2, 1, 0).reshape(1, SEQ, D_MODEL)
```

```python
import math
from contextlib import ExitStack, nullcontext

import concourse.bass as bass
from concourse import mybir
import numpy as np

F32 = mybir.dt.float32
F32R = mybir.dt.float32r
ACT = mybir.ActivationFunctionType
ALU = mybir.AluOpType
AX_X = mybir.AxisListType.X
ds = bass.ds

P = 128
D_MODEL, SEQ, CTX_LEN, DEPTH, GRID_W = 1024, 256, 256, 2, 64
TOK = CTX_LEN + SEQ
DC = D_MODEL // P
N_MOD = 9
D_FF = 2816
FT = D_FF // P
DIFF_HEADS, DIFF_HD = 4, 64
MLA_HEADS, MLA_NOPE, MLA_ROPE, MLA_VD = 8, 64, 32, 64
MLA_QD = MLA_NOPE + MLA_ROPE
Q_RANK, KV_RANK = 384, 256
QC, KVC = Q_RANK // P, KV_RANK // P
FG = 4
NB = 3
RMS_EPS = 1e-6
ROPE_BASE = 10000.0
IN_OFF = np.cumsum([0, 512, 512, 512, Q_RANK, KV_RANK, MLA_ROPE, 512])
LAM_INIT = [0.8 - 0.6 * math.exp(-0.3 * l) for l in range(DEPTH)]

RAW = 4
H = 1024
F_HALVES = [12, 10]
MODT = N_MOD * DC
CTX, LAT = slice(0, CTX_LEN), slice(CTX_LEN, TOK)
S_X, S_C = 0, 1
FREE = 2
FREE_NX = 4


WALLS = 7
ROPES = 8
PARTS = 12
DVE_LAM = 1 + DEPTH + 1
Y_TOTAL = DEPTH * (3 * DC + DIFF_HEADS + QC + KVC) + DC


def unit_plan():
    c = dict(u=0, q=0, f=0, a=0, g=0, d=0, f_all=0)
    marks, units = {}, []

    def mark(name, **k):
        marks[name] = dict(c, **k)

    def add(kind, n, w, job=True):
        for _ in range(n):
            units.append((kind, w))
        c["u"] += n
        c["q"] += n if job else 0

    mark("start")
    add("ada", 8, (1024, 1024), job=False)
    c["a"] += 4
    c["d"] += DC

    def pair(kind, ada):
        if ada:
            add("ada", 2, (1024, 1024), job=False)
            c["a"] += 1
        add(kind, 2, (1024, 1024))

    def ffn(l, k, with_ada):
        for part, nf in enumerate(F_HALVES):
            nb, first = with_ada[part], 0
            if part == 0:
                mark(("pre", l, 2 * k), ada=nb > 0)
                pair("up", nb > 0)
                c["f"] += 2
                nb, first = max(nb - 1, 0), 2
            mark(("up", l, k, part), bodies=nb, first=first)
            for _ in range(nb):
                for _ in range(2):
                    add("ada", 1, (1024, 1024), job=False)
                    add("up", 1, (1024, 1024))
                c["a"] += 1
            add("up", nf - first - 2 * nb, (1024, 1024))
            c["f"] += nf - first
            mark(("down", l, k, part))
            add(f"dn{part}", DC, (nf * 64, nf * 64))
            if part:
                c["d"] += DC

    for l in range(DEPTH):
        last = l == DEPTH - 1
        ffn(l, 0, [6, 5] if not last else [6, 3])
        mark(("pre", l, 1), ada=l == 0)
        pair("proj", l == 0)
        mark(("qkv", l))
        add("proj", 4, (1024, 1024))
        mark(("latent", l))
        add("proj", 2, (1024, 1024))
        add("kr", 1, (1024, 1024))
        mark(("mla", l))
        add("kvv", 2, (256, 256))
        for _ in range(4):
            add("uq", 1, (QC * P, QC * P))
            add("kvk", 1, (256, 256))
        mark(("four", l))
        add("proj", 2, (1024, 1024))
        mark(("merge", l))
        add("merge", DC * NB, (1024, 512))
        c["g"] += DC * NB
        mark(("wout", l))
        add("wout", DC, (512, 512))
        c["d"] += DC
        ffn(l, 1, [6, 5] if not last else [0, 0])
    mark("end")
    assert c["a"] == DEPTH * MODT // 4, c
    return marks, units


MARKS, UNITS = unit_plan()
KINDS = ["ada", "up", "dn0", "dn1", "proj", "kr", "kvv", "uq", "kvk", "merge", "wout"]


def build(nc, A):
    M = MARKS
    with ExitStack() as ctx:
        def sb(name, shape, dt=F32):
            return ctx.enter_context(nc.sbuf_tensor(name, shape, dt))

        def sem(name):
            return ctx.enter_context(nc.semaphore(name))

        x = sb("x_res", [P, DC, TOK])
        xnh = sb("xn_hi", [P, DC, TOK], F32R)
        xnl = sb("xn_lo", [P, DC, TOK], F32R)
        raw = sb("w_raw", [P, RAW, 2, H])
        wh = sb("w_hi", [P, 2, 2, H], F32R)
        wl = sb("w_lo", [P, 2, 2, H], F32R)
        R = sb("split_scratch", [P, 13312], F32R)
        S = sb("scratch", [P, 8192])
        mods = sb("mods", [P, 2, DEPTH * MODT])
        adab = sb("ada_bias", [P, DEPTH * MODT])
        cz = sb("c_split", [P, DC, 76], F32R)
        ident = sb("ident", [P, P])
        ones = sb("ones", [P, 2])
        eps = sb("eps", [P, 1])
        ada_rows = sb("ada_rows", [72, 256])
        ada_sum = sb("ada_sum", [P, 8])
        rope_d = sb("rope_d", [P, 2, SEQ])
        rope_m = sb("rope_m", [P, 2, SEQ])
        rope_t = sb("rope_tmp", [P, SEQ])
        gains = sb("gains", [P, DEPTH * 3 * DC])
        gfin = sb("gain_final", [P, DC])
        gsub = sb("gain_sub", [P, DEPTH])
        gq = sb("gain_q", [P, DEPTH * QC])
        gkv = sb("gain_kv", [P, DEPTH * KVC])
        vec = sb("vectors", [P, DC, 2])
        vsil = sb("vectors_silu", [P, DC, 2])
        amul = sb("norm_scale", [P, 2, DC])
        ghalf = sb("gate_half", [P, 2, DC])
        spare = sb("spare", [P, 1])
        sd = sb("norm_std", [P, 16])
        rs = sb("norm_rstd", [P, 16])
        nlam = sb("neg_lambda", [P, DEPTH])
        lamp = sb("lambda_parts", [P, DEPTH, 2])
        mx = sb("score_max", [P, 2, 2])
        nm = sb("score_negmax", [P, 2, 2])
        sm = sb("prob_sum", [P, 2, 2])
        rr = sb("prob_rsum", [P, 2, 2])

        ps = ctx.enter_context(nc.psum_tensor("ps", [P, 8, 512], F32))
        B_ADA, B_T, B_ST, B_RB = 4, 5, 6, 7
        B_TR, B_O, B_S = 6, 7, 4

        SA, SB, SC, SD = (S[:, 2048 * k:2048 * (k + 1)] for k in range(4))

        def v(ap, pat, **k):
            return ap.rearrange(pat, **k)

        acc = SB[:, 1024:1536]
        sq = v(SB[:, 0:1024], "p (b n) -> p b n", b=2)
        nx = v(SA, "p (b n) -> p b n", b=4)
        nx_d = v(SD, "p (b n) -> p b n", b=4)
        sil = v(SC[:, 0:1024], "p (b n) -> p b n", b=2)
        ht = v(SC[:, 1024:2048], "p (b n) -> p b n", b=2)
        hh = v(R[:, 0:6144], "p (f n) -> p f n", f=12)
        hl = v(R[:, 6144:12288], "p (f n) -> p f n", f=12)
        Qf = v(SA, "p (h n) -> p h n", h=4)
        Vt = v(SB, "p (t n) -> p t n", t=4)
        Kf = v(SC, "p (h n) -> p h n", h=4)
        Pd = v(SC, "p (b m n) -> p b m n", b=2, m=2)
        WT = v(SD, "p (b k n) -> p b k n", b=2, k=4)
        CQ = v(S[:, 4096 + 1024:4096 + 1024 + 2560], "p (c n) -> p c n", c=5)
        Pm = v(SC[:, 0:1024], "p (b n) -> p b n", b=2)
        YM = v(SA, "p (c n) -> p c n", c=4)
        YDh, YDl = (v(R[:, a:a + 2048], "p (c n) -> p c n", c=4) for a in (0, 2048))
        YMh, YMl = (v(R[:, a:a + 2048], "p (c n) -> p c n", c=4) for a in (4096, 6144))
        YFh, YFl = (v(R[:, a:a + 2048], "p (c n) -> p c n", c=4) for a in (8192, 10240))
        Kh, Kl = YMh, YMl
        QM = v(R[:, 8192:12288], "p (b m z n) -> p b m z n", b=2, m=2, z=2)
        CNh, CNl = (v(R[:, a:a + 1536], "p (c n) -> p c n", c=3) for a in (4096, 5632))
        CKh, CKl = (v(R[:, a:a + 1024], "p (c n) -> p c n", c=2) for a in (7168, 8192))
        MK = [(R[:, 9216:9728], R[:, 9728:10240]),
              (R[:, 12288:12800], R[:, 12800:13312])]
        MQ = v(R[:, 10240:12288], "p (b z n) -> p b z n", b=2, z=2)
        kr = SB[0:MLA_QD, 1536:2048]
        Ff = v(SC, "p (g n) -> p g n", g=4)
        AB = v(SB[:, 0:1024], "p (b t n) -> p b t n", b=2, t=2)
        DFT_D = SD[:, 0:256]
        DFT_C = v(SD[:, 256:768], "p (t n) -> p t n", t=2)
        DFT_S = v(SD[:, 768:1280], "p (t n) -> p t n", t=2)
        ROT_D = SD[:, 1280:1408]
        MG = v(S[:, 4096:8192], "p (m n) -> p m n", m=DC)
        sig = v(SA[:, 0:1024], "p (b n) -> p b n", b=2)
        prod = v(SA[:, 1024:2048], "p (b n) -> p b n", b=2)
        out_y = v(SC, "p (m n) -> p m n", m=DC)

        raw_loaded = [sem(f"raw_loaded{k}") for k in range(RAW)]
        c_loaded = sem("c_loaded")
        x_loaded = sem("x_loaded")
        consts_loaded = sem("consts_loaded")
        tables_loaded = sem("tables_loaded")
        out_stored = sem("out_stored")
        hi_ready = sem("hi_ready")
        split_ready = sem("split_ready")
        half_used = sem("half_used")
        psum_free = sem("psum_free")
        silu_ready = sem("silu_ready")
        hhi_ready = sem("hhi_ready")
        h_ready = sem("h_ready")
        sq_ready = sem("sq_ready")
        acc_ready = sem("acc_ready")
        ada_staged = sem("ada_staged")
        ada_turned = sem("ada_turned")
        ada_summed = sem("ada_summed")
        mods_ready = sem("mods_ready")
        setup_ready = sem("setup_ready")
        stat_done = sem("stat_done")
        std_ready = sem("std_ready")
        rstd_ready = sem("rstd_ready")
        rb_ready = sem("rb_ready")
        rb_used = sem("rb_used")
        y_ready = sem("y_ready")
        yhi_ready = sem("yhi_ready")
        ylo_ready = sem("ylo_ready")
        sig_ready = sem("sig_ready")
        merge_ready = sem("merge_ready")
        rot_done = sem("rot_done")
        rot_used = sem("rot_used")
        part_hi = sem("part_hi")
        part_lo = sem("part_lo")
        qhi_ready = sem("qhi_ready")
        q_ready = sem("q_ready")
        qk_done = sem("qk_done")
        negmax_ready = sem("negmax_ready")
        exp_done = sem("exp_done")
        w_ready = sem("w_ready")
        tr_done = sem("tr_done")
        wt_ready = sem("wt_ready")
        pv_done = sem("pv_done")
        o_ready = sem("o_ready")
        ab_done = sem("ab_done")
        ab_ready = sem("ab_ready")
        yf_done = sem("yf_done")
        yf_hi = sem("yf_hi")
        yf_ready = sem("yf_ready")
        nt_ready = sem("nt_ready")
        mq_ready = sem("mq_ready")
        dve_chain = sem("dve_chain")
        act_chain = sem("act_chain")
        pool_chain = sem("pool_chain")
        phase_end = {e: sem(f"phase_end_{e}") for e in ("pe", "act", "dve", "pool")}

        block = ctx.enter_context(nc.Block())

        def streams(both):
            return [(CTX, S_C), (LAT, S_X)] if both else [(LAT, S_X)]

        def width(both):
            return slice(0, TOK) if both else LAT

        def phase_wall(eng, me, walls):
            eng.drain().then_inc(phase_end[me], 1)
            walls[0] += 1
            for other in phase_end:
                if other != me:
                    eng.wait_ge(phase_end[other], walls[0])

        def ahead(u, per, n):
            ws = [UNITS[u + per * i][1] for i in range(n) if u + per * i < len(UNITS)]
            return max(w[0] for w in ws), max(w[1] for w in ws)

        def up_runs(l, k, part):
            m = M[("up", l, k, part)]
            u, q, f, a, n = m["u"], m["q"], m["f"], m["a"], m["bodies"]
            out = []
            if n:
                out.append((u, q, f, a, ("ada", "up") * 2, n))
                u, q, f = u + 4 * n, q + 2 * n, f + 2 * n
            left = F_HALVES[part] - m["first"] - 2 * n
            if left // 4:
                out.append((u, q, f, None, ("up",) * 4, left // 4))
                u, q, f = u + left // 4 * 4, q + left // 4 * 4, f + left // 4 * 4
            if left % 4:
                out.append((u, q, f, None, ("up",) * (left % 4), 1))
            return out

        def loop(eng, n):
            return eng.Fori(0, n) if n > 1 else nullcontext(0)

        def item_list(l, heads):
            items, pairs = [], []
            for h in range(heads):
                for cols, nk in [(LAT, TOK)] + ([(CTX, CTX_LEN)] if l < DEPTH - 1 else []):
                    for t in range(2):
                        items.append((h, len(pairs), t, cols.start + t * P, nk))
                    pairs.append((h, cols, nk))
            return items, pairs

        def mla_extras(l, t):
            per = 2 * len(item_list(l, 1)[0])
            i, s = divmod(t, per)
            head = 2 * i + 2 if s == per // 2 else 2 * i + 3 if s == per - 1 else None
            halves = [(i + 1, p) for p in range(4) if s == per * p // 8 and i + 1 < MLA_HEADS // 2]
            return (head if head is not None and head < MLA_HEADS else None), halves

        def head_squares(h):
            return SC[:, 512 * h:512 * (h + 1)]

        @block.sync
        def _(sp):
            at = {k: 0 for k in KINDS}
            W = (1024, 1024)

            def load_units(u0, body, n=1):
                per = {k: sum(b[0] == k for b in body) for k, _ in body}
                assert n == 1 or (len(body) % RAW == 0 and u0 >= RAW)
                with loop(sp, n) as i:
                    seen = dict.fromkeys(per, 0)
                    for j, (kind, w) in enumerate(body):
                        u, nth = u0 + j, at[kind] + seen[kind]
                        seen[kind] += 1
                        slot = u % RAW
                        if u >= RAW:
                            sp.wait_ge(split_ready, 2 * (u - RAW) + 2 + i * (2 * len(body)))
                        src = A[kind][nth] if n == 1 else \
                            A[kind][ds(i * per[kind] + nth, 1)].rearrange("a p n -> p (a n)")
                        if w[0] == w[1]:
                            dst = raw[:, slot, :, 0:w[0]]
                            src = src.rearrange("p (h n) -> p h n", h=2)
                        else:
                            dst = raw[:, slot].rearrange("p h n -> p (h n)")[:, 0:w[0] + w[1]]
                        sp.dma_start(dst, src).then_inc(raw_loaded[slot], 16)
                for k in per:
                    at[k] += per[k] * n

            sp.dma_start(vec[:], A["vec"]).then_inc(c_loaded, 16)
            sp.dma_start(adab[:], A["ada_b"]).then_inc(c_loaded, 16)
            load_units(0, [("ada", W)] * 2)
            sp.dma_start(x[:, :, CTX], A["ctxT"]).then_inc(x_loaded, 16)
            sp.dma_start(x[:, :, LAT], A["xT"]).then_inc(x_loaded, 16)
            load_units(2, [("ada", W)] * 2)
            for dst, src in ((gains[:], A["norm_g"]),
                             (gfin[:], A["final_g"]), (gsub[:], A["sub_g"]), (gq[:], A["q_g"]),
                             (gkv[:], A["kv_g"]), (rope_d[:], A["rope_d"]), (rope_m[:], A["rope_m"]),
                             (SD[:, 0:512], A["lam"])):
                sp.dma_start(dst, src).then_inc(consts_loaded, 16)
            load_units(4, [("ada", W)] * 4)

            def load_pair(l, k, kind):
                m = M[("pre", l, k)]
                load_units(m["u"], [("ada", W)] * (2 * m["ada"]) + [(kind, W)] * 2)

            def load_ffn(l, k):
                load_pair(l, 2 * k, "up")
                for part, nf in enumerate(F_HALVES):
                    for u, _, _, _, body, n in up_runs(l, k, part):
                        load_units(u, [(kind, W) for kind in body], n)
                    load_units(M[("down", l, k, part)]["u"], [(f"dn{part}", (nf * 64,) * 2)] * 4, DC // 4)

            for l in range(DEPTH):
                load_ffn(l, 0)
                load_pair(l, 1, "proj")
                load_units(M[("qkv", l)]["u"], [("proj", W)] * 4)
                for e in phase_end:
                    sp.wait_ge(phase_end[e], WALLS * l + 1)
                sp.dma_start(ROT_D, A["rot_d"]).then_inc(tables_loaded, 16)
                load_units(M[("latent", l)]["u"], [("proj", W)] * 2 + [("kr", W)]
                           + [("kvv", (256, 256))] * 2 + [("uq", (QC * P,) * 2), ("kvk", (256, 256))] * 4)
                load_units(M[("four", l)]["u"], [("proj", W)] * 2)
                for e in phase_end:
                    sp.wait_ge(phase_end[e], WALLS * l + 6)
                sp.dma_start(SD[:, 0:1280], A["dft"]).then_inc(tables_loaded, 16)
                load_units(M[("merge", l)]["u"], [("merge", (1024, 512))] * 12, 2)
                load_units(M[("wout", l)]["u"], [("wout", (512, 512))] * 4, DC // 4)
                load_ffn(l, 1)
            sp.wait_ge(y_ready, Y_TOTAL)
            sp.dma_start(A["out"], out_y).then_inc(out_stored, 16)
            sp.wait_ge(out_stored, 16)

        @block.tensor
        def _(pe):
            walls, done = [0], dict(norm=0, group=0, chunk=0, item=0, pair=0, rot=0, part=0, head=0,
                                    four=0)

            def half(u, h, i=0, per=0):
                pe.wait_ge(split_ready, 2 * u + h + 1 + i * (2 * per))

            def pair_free(q, i=0, per=0):
                pe.wait_ge(psum_free, FREE + q - 1 + i * per)
                return 2 * (q % 2)

            def product(out, wtile, hi, lo, first, last, m=P):
                w_hi, w_lo = wtile
                nc.tensor.matmul(out, w_hi, hi, start=first, stop=False)
                nc.tensor.matmul(out, w_lo, hi, start=False, stop=False)
                return nc.tensor.matmul(out, w_hi, lo, start=False, stop=last)

            def wtile(u, h, k, n=P):
                cols = slice(k * n, (k + 1) * n)
                return wh[:, u % 2, h, cols], wl[:, u % 2, h, cols]

            def feature_tile(u, h, out, k0, nk, first, last, hi, lo, cols, n=P):
                for kk in range(nk):
                    ins = product(out, wtile(u, h, kk, n), hi[:, k0 + kk, cols], lo[:, k0 + kk, cols],
                                  first and kk == 0, last and kk == nk - 1)
                return ins

            def ada_unit(u, un, a, i=0, per=0):
                if un == 0:
                    pe.wait_ge(ada_staged, a + i)
                for h in range(2):
                    half(u, h, i, per)
                    for kk in range(4):
                        c = cz[:, 4 * h + kk, 4:76] if un == 0 else cz[:, 4 * h + kk, 0:72]
                        cols = slice(256 * kk, 256 * kk + 256)
                        nc.tensor.matmul(ps[0:72, B_ADA, 0:256], c, wh[:, u % 2, h, cols],
                                         start=(un == h == kk == 0), stop=False)
                        ins = nc.tensor.matmul(ps[0:72, B_ADA, 0:256], c, wl[:, u % 2, h, cols],
                                               start=False, stop=(un == 1 and h == 1 and kk == 3))
                    ins.then_inc(half_used, 1)

            def ada_turn(a, i=0):
                pe.wait_ge(ada_staged, a + 1 + i)
                pe.wait_ge(mods_ready, a + i)
                for cb in range(2):
                    ins = nc.tensor.transpose(ps[:, B_T, 72 * cb:72 * cb + 72],
                                              ada_rows[:, cb * P:(cb + 1) * P], ident[0:72, 0:72])
                ins.then_inc(ada_turned, 1)

            def norm(groups):
                k = 0
                for sums, cols, nch in groups:
                    for t in range(cols.start, cols.stop, P):
                        ins = nc.tensor.matmul(ps[:, B_ST, 2 * k:2 * k + 2], sums[:, t:t + P], ones[:],
                                               start=True, stop=True)
                        k += 1
                done["norm"] += 1
                ins.then_inc(stat_done, 1)
                pe.wait_ge(rstd_ready, done["norm"])
                k = 0
                for sums, cols, nch in groups:
                    pe.wait_ge(rb_used, FREE + done["group"] - 1)
                    bank = (B_RB, B_ADA)[done["group"] % 2]
                    for t in range(cols.start, cols.stop, P):
                        ins = nc.tensor.matmul(ps[:, bank, t:t + P], rs[:, k:k + 1].to_broadcast([P, P]),
                                               ident[:], start=True, stop=True)
                        k += 1
                    done["group"] += 1
                    ins.then_inc(rb_ready, 1)
                    done["chunk"] += nch

            def x_norm(l, k):
                m = M["start"] if (l, k) == (0, 0) else M[("down", l - 1, 1, 1) if k == 0 else
                                                          ("down", l, 0, 1) if k == 1 else ("wout", l)]
                pe.wait_ge(acc_ready, FREE + m["d"] + DC)
                norm([(acc, width(l < DEPTH - 1 or k < 2), DC)])

            def norm_and_pair(l, k):
                m = M[("pre", l, k)]
                u, q = m["u"], m["q"]
                if m["ada"]:
                    ada_unit(u, 0, m["a"])
                    ada_unit(u + 1, 1, m["a"])
                    u += 2
                c0 = done["chunk"]
                x_norm(l, k)
                if m["ada"]:
                    ada_turn(m["a"])
                cols = width(l < DEPTH - 1 or k == 0)
                pair_free(q)
                pair_free(q + 1)
                for h in range(2):
                    half(u, h)
                    half(u + 1, h)
                for c in range(DC):
                    pe.wait_ge(ylo_ready, FREE_NX + c0 + c + 1)
                    for j in range(2):
                        for h in range(2):
                            ins = product(ps[:, 2 * ((q + j) % 2) + h, cols], wtile(u + j, h, c), xnh[:, c, cols],
                                          xnl[:, c, cols], c == 0, c == DC - 1)
                            if c == DC - 1:
                                ins.then_inc(half_used, 1)

            def ffn(l, k):
                both = l < DEPTH - 1 or k == 0
                cols = width(both)
                for part, nf in enumerate(F_HALVES):
                    for u0, q0, f0, a0, body, n in up_runs(l, k, part):
                        per, jobs = len(body), body.count("up")
                        with loop(pe, n) as i:
                            j = 0
                            for p, kind in enumerate(body):
                                u = u0 + p
                                if kind == "ada":
                                    ada_unit(u, p // 2, a0, i, per)
                                    continue
                                b = pair_free(q0 + j, i, jobs)
                                for h in range(2):
                                    half(u, h, i, per)
                                    feature_tile(u, h, ps[:, b + h, cols], 0, DC, True, True, xnh, xnl, cols
                                                 ).then_inc(half_used, 1)
                                j += 1
                            if a0 is not None:
                                ada_turn(a0, i)
                    m = M[("down", l, k, part)]
                    pe.wait_ge(h_ready, FREE + m["f"] - 1)
                    with loop(pe, DC // 4) as i:
                        for j in range(4):
                            u = m["u"] + j
                            b = pair_free(m["q"] + j, i, 4)
                            for h in range(2):
                                half(u, h, i, 4)
                                for kk in range(nf // 2):
                                    c = h * (nf // 2) + kk
                                    if c == nf - 1:
                                        pe.wait_ge(h_ready, FREE + m["f"])
                                    ins = product(ps[:, b, cols], wtile(u, h, kk), hh[:, c, cols], hl[:, c, cols],
                                                  c == 0, c == nf - 1)
                                ins.then_inc(half_used, 1)

            def proj(u, q, cols0, cols1=None):
                b = pair_free(q)
                for h, cols in ((0, cols0), (1, cols1 or cols0)):
                    half(u, h)
                    feature_tile(u, h, ps[:, b + h, cols], 0, DC, True, True, xnh, xnl, cols).then_inc(half_used, 1)

            def proj_tokens(u, q, k, hi, lo, then=None):
                b = pair_free(q)
                half(u, 0)
                half(u, 1)
                for t in range(TOK // P):
                    rows = slice(t * P, (t + 1) * P)
                    out = ps[:, b + t // 2, (t % 2) * 256:(t % 2) * 256 + 256]
                    for h in range(2):
                        for kk in range(k // 2):
                            c = h * (k // 2) + kk
                            w = slice(kk * 256, kk * 256 + 256)
                            ins = nc.tensor.matmul(out, hi[:, c, rows], wh[:, u % 2, h, w],
                                                   start=(c == 0), stop=False)
                            ins = nc.tensor.matmul(out, hi[:, c, rows], wl[:, u % 2, h, w], start=False, stop=False)
                            ins = nc.tensor.matmul(out, lo[:, c, rows], wh[:, u % 2, h, w],
                                                   start=False, stop=(c == k - 1))
                    if t == TOK // P - 1:
                        ins.then_inc(half_used, 2)
                    if then:
                        then(t)

            def rotate(bank, off, table, src):
                n = src.shape[0]
                done["rot"] += 1
                nc.tensor.matmul(ps[0:n, bank, off:off + SEQ], table, src, start=True, stop=True
                                 ).then_inc(rot_done, 1)

            def transposes(a, nk, src):
                pe.wait_ge(w_ready, a + 1)
                pe.wait_ge(wt_ready, a)
                for kc in range(nk // P):
                    ins = nc.tensor.transpose(ps[:, B_TR, kc * P:(kc + 1) * P], src[:, kc * P:(kc + 1) * P], ident[:])
                ins.then_inc(tr_done, 1)

            def outputs(a, g, nk, rows, vcols):
                pe.wait_ge(wt_ready, a + 1)
                pe.wait_ge(o_ready, g)
                for kc in range(nk // P):
                    ins = nc.tensor.matmul(ps[rows, B_O, 0:256], Vt[:, kc, vcols], WT[:, g % 2, kc, :],
                                           start=(kc == 0), stop=(kc == nk // P - 1))
                ins.then_inc(pv_done, 1)

            def diff_attention(l):
                items, pairs = item_list(l, DIFF_HEADS)
                a0, g0 = done["item"], done["pair"]

                def scores(t):
                    h, g, _, col, nk = items[t]
                    if t == 0 or items[t - 1][0] != h:
                        pe.wait_ge(q_ready, done["head"] + h + 1)
                    if a0 + t >= 2:
                        pe.wait_ge(exp_done, a0 + t - 1)
                    for m in range(2):
                        q_hi, q_lo = (QM[:, h % 2, m, z, col:col + P] for z in range(2))
                        out = ps[:, 2 * (t % 2) + m, 0:nk]
                        nc.tensor.matmul(out, q_hi, Kh[:, h, 0:nk], start=True, stop=False)
                        nc.tensor.matmul(out, q_lo, Kh[:, h, 0:nk], start=False, stop=False)
                        ins = nc.tensor.matmul(out, q_hi, Kl[:, h, 0:nk], start=False, stop=True)
                    ins.then_inc(qk_done, 1)

                scores(0)
                for t in range(len(items) + 3):
                    if t + 1 < len(items):
                        scores(t + 1)
                    if 0 <= t - 2 < len(items):
                        transposes(a0 + t - 2, items[t - 2][4], Pd[:, t % 2, 0])
                    if t >= 3 and items[t - 3][2] == 1:
                        h, g, _, _, nk = items[t - 3]
                        outputs(a0 + t - 3, g0 + g, nk, slice(0, P), slice(h * P, (h + 1) * P))
                done["item"] += len(items)
                done["pair"] += len(pairs)
                done["head"] += DIFF_HEADS

            def mla_half(l, i, p):
                m = M[("mla", l)]
                u, q = m["u"] + 2 + 2 * i, m["q"] + 2 + 2 * i
                h = p % 2
                if p < 2:
                    b, cols, k, hi, lo = pair_free(q), width(l < DEPTH - 1), QC, CNh, CNl
                else:
                    b, cols, k, hi, lo = pair_free(q + 1), slice(0, TOK), KVC, CKh, CKl
                half(u + p // 2, h)
                feature_tile(u + p // 2, h, ps[:, b + h, cols], 0, k, True, True, hi, lo, cols).then_inc(half_used, 1)

            def mla_attention(l):
                items, pairs = item_list(l, MLA_HEADS)
                a0, g0 = done["item"], done["pair"]
                for p in range(4):
                    mla_half(l, 0, p)

                def scores(t):
                    h, g, _, col, nk = items[t]
                    MKh, MKl = MK[h % 2]
                    if t == 0 or items[t - 1][0] != h:
                        pe.wait_ge(q_ready, done["head"] + h + 1)
                    pe.wait_ge(exp_done, a0 + t - 1)
                    q_hi, q_lo = (MQ[0:MLA_QD, h % 2, z, col:col + P] for z in range(2))
                    out = ps[:, B_S + t % 2, 0:nk]
                    nc.tensor.matmul(out, q_hi, MKh[0:MLA_QD, 0:nk], start=True, stop=False)
                    nc.tensor.matmul(out, q_lo, MKh[0:MLA_QD, 0:nk], start=False, stop=False)
                    nc.tensor.matmul(out, q_hi, MKl[0:MLA_QD, 0:nk], start=False, stop=True).then_inc(qk_done, 1)

                scores(0)
                for t in range(len(items) + 3):
                    if t + 1 < len(items):
                        scores(t + 1)
                    if 0 <= t - 2 < len(items):
                        transposes(a0 + t - 2, items[t - 2][4], Pm[:, t % 2])
                    if t >= 3 and items[t - 3][2] == 1:
                        h, g, _, _, nk = items[t - 3]
                        outputs(a0 + t - 3, g0 + g, nk, slice(64 * (h % 2), 64 * (h % 2) + 64),
                                slice(h * MLA_VD, (h + 1) * MLA_VD))
                    if t < len(items):
                        for i, p in mla_extras(l, t)[1]:
                            mla_half(l, i, p)
                done["item"] += len(items)
                done["pair"] += len(pairs)
                done["head"] += MLA_HEADS

            def fourier(l):
                m = M[("four", l)]
                both = l < DEPTH - 1
                for j in range(2):
                    proj(m["u"] + j, m["q"] + j, width(both))
                pe.wait_ge(psum_free, FREE + m["q"] + 2)
                pe.wait_ge(tables_loaded, 16 * (2 * l + 2))
                jobs = [(g, cols) for g in range(FG) for cols, _ in streams(both)]
                k0 = done["four"]
                for t in range(len(jobs) + 1):
                    if t < len(jobs):
                        g, cols = jobs[t]
                        if k0 + t >= 2:
                            pe.wait_ge(ab_ready, k0 + t - 1)
                        for tt in range(2):
                            c = cols.start + tt * P
                            ins = nc.tensor.matmul(ps[:, 4 + t % 2, tt * 256:tt * 256 + 256], Ff[:, g, c:c + P],
                                                   DFT_D, start=True, stop=True)
                        ins.then_inc(ab_done, 1)
                    if t >= 1:
                        pe.wait_ge(ab_ready, k0 + t)
                        if k0 + t - 1 >= 2:
                            pe.wait_ge(yf_ready, k0 + t - 2)
                        b = (t - 1) % 2
                        for tt in range(2):
                            nc.tensor.matmul(ps[:, 6 + b, 0:SEQ], AB[:, b, tt, 0:P], DFT_C[:, tt, :],
                                             start=(tt == 0), stop=False)
                            ins = nc.tensor.matmul(ps[:, 6 + b, 0:SEQ], AB[:, b, tt, P:2 * P], DFT_S[:, tt, :],
                                                   start=False, stop=(tt == 1))
                        ins.then_inc(yf_done, 1)
                done["four"] += len(jobs)

            pe.wait_ge(setup_ready, 1)
            pe.wait_ge(acc_ready, FREE)
            for a in range(4):
                ada_unit(2 * a, 0, a)
                ada_unit(2 * a + 1, 1, a)
                ada_turn(a)
            for l in range(DEPTH):
                both = l < DEPTH - 1
                norm_and_pair(l, 0)
                ffn(l, 0)
                norm_and_pair(l, 1)
                phase_wall(pe, "pe", walls)
                m = M[("qkv", l)]
                u, q = m["u"], m["q"]
                for j in range(2):
                    proj(u + j, q + j, slice(0, TOK))

                def rotation(c):
                    if c == 0:
                        pe.wait_ge(psum_free, FREE + q + 2)
                        pe.wait_ge(tables_loaded, 16 * (2 * l + 1))
                        pe.wait_ge(mods_ready, m["a"])
                    if c >= 2:
                        pe.wait_ge(rot_used, ROPES * l + c - 1)
                    rotate(4 + c % 2, 0, ROT_D, (Qf if c < 4 else Kf)[:, c % 4, LAT])

                for j in range(2):
                    proj_tokens(u + 2 + j, q + 2 + j, DC, xnh, xnl, lambda t: rotation(4 * j + t))
                phase_wall(pe, "pe", walls)
                diff_attention(l)
                phase_wall(pe, "pe", walls)
                pe.wait_ge(part_lo, PARTS * l + 5)
                norm([(head_squares(h), width(both), 1) for h in range(DIFF_HEADS)])
                phase_wall(pe, "pe", walls)
                m = M[("latent", l)]
                u, q = m["u"], m["q"]
                proj(u, q, width(both))
                proj(u + 1, q + 1, width(both), slice(0, TOK))
                proj(u + 2, q + 2, slice(0, TOK))
                pe.wait_ge(part_lo, PARTS * l + 6)
                norm([(SB[:, 0:512], width(both), QC), (SB[:, 512:1024], slice(0, TOK), KVC)])
                phase_wall(pe, "pe", walls)
                pe.wait_ge(ylo_ready, FREE_NX + done["chunk"])
                m = M[("mla", l)]
                for j in range(2):
                    proj_tokens(m["u"] + j, m["q"] + j, KVC, CKh, CKl)
                mla_attention(l)
                phase_wall(pe, "pe", walls)
                fourier(l)
                phase_wall(pe, "pe", walls)
                m = M[("merge", l)]
                cols = width(both)
                ys = ((YDh, YDl), (YMh, YMl), (YFh, YFl))
                with loop(pe, 2) as i:
                    for j in range(12):
                        u, (yh, yl) = m["u"] + j, ys[j % NB]
                        b = pair_free(m["q"] + j, i, 12)
                        half(u, 0, i, 12)
                        feature_tile(u, 0, ps[:, b, cols], 0, DC, True, True, xnh, xnl, cols).then_inc(half_used, 1)
                        half(u, 1, i, 12)
                        feature_tile(u, 1, ps[:, b + 1, cols], 0, 4, True, True, yh, yl, cols).then_inc(half_used, 1)
                m = M[("wout", l)]
                pair_free(m["q"])
                pair_free(m["q"] + 1)
                for c in range(DC):
                    pe.wait_ge(ylo_ready, FREE_NX + done["chunk"] + c + 1)
                    for j in range(2):
                        u, h = m["u"] + j, c // 4
                        if c % 4 == 0:
                            half(u, h)
                        ins = product(ps[:, 2 * ((m["q"] + j) % 2), cols], wtile(u, h, c % 4), xnh[:, c, cols],
                                      xnl[:, c, cols], c == 0, c == DC - 1)
                        if c % 4 == 3 and (j == 0 or h):
                            ins.then_inc(half_used, 1 + j)
                done["chunk"] += DC
                for j in range(2, DC):
                    u = m["u"] + j
                    b = pair_free(m["q"] + j)
                    for h in range(2):
                        half(u, h)
                        feature_tile(u, h, ps[:, b, cols], 4 * h, 4, h == 0, h == 1, xnh, xnl, cols
                                     ).then_inc(half_used, 1)
                norm_and_pair(l, 2)
                ffn(l, 1)
            pe.wait_ge(acc_ready, FREE + M["end"]["d"])
            norm([(acc, LAT, DC)])

        @block.scalar
        def _(act):
            walls, done = [0], dict(norm=0, y=0, item=0, pair=0, four=0, chain=0)

            def link(ins):
                done["chain"] += 1
                ins.then_inc(act_chain, 1)
                act.wait_ge(act_chain, done["chain"])

            def round_half(u, h, i=0, per=0, n=1):
                if u >= len(UNITS):
                    return
                w = ahead(u, per, n)[h]
                if h == 0:
                    act.wait_ge(raw_loaded[u % RAW], 16 * (u // RAW + 1) + i * (16 * per // RAW))
                if 2 * u + h >= 4:
                    act.wait_ge(half_used, 2 * u + h - 3 + i * (2 * per))
                nc.scalar.copy(wh[:, u % 2, h, 0:w], raw[:, u % RAW, h, 0:w]).then_inc(hi_ready, 1)

            def round_unit(u, i=0, per=0, n=1):
                for h in range(2):
                    round_half(u, h, i, per, n)

            def used(u, h, i=0, per=0):
                act.wait_ge(half_used, 2 * u + h + 1 + i * (2 * per))

            def ada_stage(u, a, i=0, per=0):
                used(u, 1, i, per)
                act.wait_ge(ada_turned, a + i)
                nc.scalar.copy(ada_rows[:], ps[0:72, B_ADA, 0:256]).then_inc(ada_staged, 1)

            def square(d, cols, b, m, i=0):
                act.wait_ge(acc_ready, FREE + d - 1 + i)
                nc.scalar.activation(sq[:, b, cols], x[:, m, cols], ACT.Square).then_inc(sq_ready, 1)

            def sqrt_table():
                act.wait_ge(rstd_ready, done["norm"])
                link(nc.scalar.activation(spare[:], eps[:], ACT.Sqrt))

            def norm(groups, chunks, tmp=None, ahead_=False):
                if not ahead_:
                    sqrt_table()
                done["norm"] += 1
                act.wait_ge(stat_done, done["norm"])
                k = 0
                for n, (cols, dim) in enumerate(groups):
                    nt_ = (cols.stop - cols.start) // P
                    ins = nc.scalar.activation(sd[:, k:k + nt_], ps[:, B_ST, 2 * k:2 * (k + nt_):2], ACT.Sqrt,
                                               bias=eps[:], scale=1.0 / dim)
                    k += nt_
                ins.then_inc(std_ready, 1)
                if callable(chunks):
                    with act.Fori(0, DC // 4) as i:
                        for j in range(4):
                            round_chunk(*chunks(i * 4 + j, j), i * 4 + j, nx)
                    done["y"] += DC
                else:
                    for b, dst, cols in chunks:
                        round_chunk(b, dst, cols, 0, tmp)
                        done["y"] += 1

            def round_chunk(b, dst, cols, c, y):
                act.wait_ge(y_ready, done["y"] + 1 + c)
                nc.scalar.copy(dst[:, cols], y[:, b, cols]).then_inc(yhi_ready, 1)

            def x_norm(l, k):
                both = l < DEPTH - 1 or k < 2
                cols = width(both)
                act.wait_ge(half_used, 2 * M[("pre", l, k)]["u"])
                norm([(cols, D_MODEL)], lambda c, j: (j, xnh[:, ds(c, 1), :].rearrange("p a n -> p (a n)"), cols),
                     ahead_=True)

            def norm_and_pair(l, k):
                m = M[("pre", l, k)]
                sqrt_table()
                if m["ada"]:
                    round_unit(m["u"] + 2)
                    round_unit(m["u"] + 3)
                    ada_stage(m["u"] + 1, m["a"])
                x_norm(l, k)

            def hidden(u, q, f, fl, cols, i=0, per=0, jobs=0, n=1):
                b = f % 2
                round_half(u + 2, 0, i, per, n)
                used(u, 0, i, per)
                act.wait_ge(psum_free, FREE + q - 1 + i * jobs)
                nc.scalar.activation(sil[:, b, cols], ps[:, 2 * (q % 2), cols], ACT.Silu).then_inc(silu_ready, 1)
                round_half(u + 2, 1, i, per, n)
                act.wait_ge(psum_free, FREE + q + 1 + i * jobs)
                nc.scalar.copy(tile(hh, i * jobs + fl)[:, cols], ht[:, b, cols]).then_inc(hhi_ready, 1)

            def ffn(l, k):
                both = l < DEPTH - 1 or k == 0
                cols = width(both)
                pre = M[("pre", l, 2 * k)]
                for j in range(2):
                    hidden(pre["u"] + 2 * pre["ada"] + j, pre["q"] + j, pre["f"] + j, j, cols)
                for part, nf in enumerate(F_HALVES):
                    for u0, q0, f0, a0, body, n in up_runs(l, k, part):
                        per, jobs = len(body), body.count("up")
                        fl0 = f0 - (pre["f"] if part == 0 else M[("up", l, k, part)]["f"])
                        with loop(act, n) as i:
                            j = 0
                            for p, kind in enumerate(body):
                                u = u0 + p
                                if kind == "ada":
                                    round_unit(u + 2, i, per, n)
                                    if p // 2:
                                        ada_stage(u, a0, i, per)
                                    continue
                                hidden(u, q0 + j, f0 + j, fl0 + j, cols, i, per, jobs, n)
                                j += 1
                    m = M[("down", l, k, part)]
                    down(m, cols, part == 1)

            def tile(t, c):
                return t[:, c, :] if isinstance(c, int) else t[:, ds(c, 1), :].rearrange("p a n -> p (a n)")

            def down(m, cols, final):
                end = m["u"] + DC >= len(UNITS)
                for first, n in ([(0, 1), (4, 1)] if end else [(0, DC // 4)]):
                    with loop(act, n) as i:
                        for j in range(first, first + 4):
                            u, q, d = m["u"] + j, m["q"] + j, m["d"] + j
                            round_unit(u + 2, i, 4, n)
                            if final:
                                act.wait_ge(psum_free, FREE + q + 1 + i * 4)
                                act.wait_ge(acc_ready, FREE + d - 1 + i * 4)
                                nc.scalar.activation(sq[:, j % 2, cols], tile(x, i * 4 + j)[:, cols], ACT.Square
                                                     ).then_inc(sq_ready, 1)

            def scores_exp(a, banks, dst, scale, nk):
                act.wait_ge(negmax_ready, a + 1)
                if a >= 2:
                    act.wait_ge(tr_done, a - 1)
                for m, bank in enumerate(banks):
                    ins = nc.scalar.activation(dst[m][:, 0:nk], ps[:, bank, 0:nk], ACT.Exp, bias=nm[:, a % 2, m:m + 1],
                                               scale=scale, accum_out=sm[:, a % 2, m:m + 1])
                ins.then_inc(exp_done, 1)

            def copy_transposed(a, g, t, nk):
                act.wait_ge(tr_done, a + 1)
                if g >= 2:
                    act.wait_ge(pv_done, g - 1)
                nc.scalar.copy(WT[:, g % 2, 0:nk // P, t * P:(t + 1) * P],
                               ps[:, B_TR, 0:nk].rearrange("p (k n) -> p k n", n=P)).then_inc(wt_ready, 1)

            def diff_q(l, h):
                cols = width(l < DEPTH - 1)
                if h >= 2:
                    act.wait_ge(qk_done, done["item"] + (h - 1) * len(item_list(l, 1)[0]))
                nc.scalar.copy(QM[0:64, h % 2, 0, 0, cols], Qf[0:64, h, cols])
                nc.scalar.copy(QM[64:P, h % 2, 1, 0, cols], Qf[64:P, h, cols]).then_inc(qhi_ready, 1)

            def diff_attention(l):
                items, pairs = item_list(l, DIFF_HEADS)
                a0, g0 = done["item"], done["pair"]
                diff_q(l, 0)
                for t in range(len(items) + 2):
                    if t < len(items):
                        h, g, _, col, nk = items[t]
                        scores_exp(a0 + t, (2 * (t % 2), 2 * (t % 2) + 1), [Pd[:, t % 2, m] for m in range(2)],
                                   DIFF_HD ** -0.5, nk)
                        if (t == 0 or items[t - 1][0] != h) and h + 1 < DIFF_HEADS:
                            diff_q(l, h + 1)
                    if t >= 2:
                        h, g, tq, _, nk = items[t - 2]
                        copy_transposed(a0 + t - 2, g0 + g, tq, nk)
                done["item"] += len(items)
                done["pair"] += len(pairs)

            def mla_qk(l, h):
                m = M[("mla", l)]
                cols = width(l < DEPTH - 1)
                i, j = h // 2, h % 2
                u, q = m["u"] + 2 + 2 * i, m["q"] + 2 + 2 * i
                if h >= 2:
                    act.wait_ge(qk_done, done["item"] + (h - 1) * len(item_list(l, 1)[0]))
                act.wait_ge(mq_ready, MLA_HEADS * l + h + 1)
                nc.scalar.copy(MQ[0:MLA_QD, j, 0, cols], ps[0:MLA_QD, 2 * (q % 2) + j, cols])
                used(u + 1, j)
                nc.scalar.copy(MK[j][0][0:64, :], ps[0:64, 2 * ((q + 1) % 2) + j, :]).then_inc(qhi_ready, 1)

            def mla_round(l, i, p):
                round_half(M[("mla", l)]["u"] + 2 + 2 * i + p // 2 + 2, p % 2)

            def mla_attention(l):
                items, pairs = item_list(l, MLA_HEADS)
                a0, g0 = done["item"], done["pair"]
                for p in range(4):
                    mla_round(l, 0, p)
                mla_qk(l, 0)
                mla_qk(l, 1)
                for t in range(len(items) + 2):
                    head, halves = mla_extras(l, t) if t < len(items) else (None, [])
                    if t < len(items):
                        scores_exp(a0 + t, (B_S + t % 2,), [Pm[:, t % 2]], MLA_QD ** -0.5, items[t][4])
                    if head is not None:
                        mla_qk(l, head)
                    if t >= 2:
                        h, g, tq, _, nk = items[t - 2]
                        copy_transposed(a0 + t - 2, g0 + g, tq, nk)
                    for i, p in halves:
                        mla_round(l, i, p)
                done["item"] += len(items)
                done["pair"] += len(pairs)

            act.wait_ge(c_loaded, 32)
            link(nc.scalar.activation(vsil[:], vec[:], ACT.Silu))
            act.wait_ge(dve_chain, 1)
            link(nc.scalar.copy(cz[:, :, 4:8:2], vsil[:]))
            round_unit(0)
            round_unit(1)
            for a in range(4):
                round_unit(2 * a + 2)
                round_unit(2 * a + 3)
                ada_stage(2 * a + 1, a)
                if a == 1:
                    act.wait_ge(x_loaded, 32)
                if a:
                    for c in range(4 * a - 4, min(4 * a, DC)):
                        act.wait_ge(acc_ready, FREE + c - 1)
                        nc.scalar.activation(sq[:, c % 2, :], x[:, c, :], ACT.Square).then_inc(sq_ready, 1)
            act.wait_ge(dve_chain, DVE_LAM)
            link(nc.scalar.activation(lamp[:], lamp[:], ACT.Exp))

            for l in range(DEPTH):
                both = l < DEPTH - 1
                cols = width(both)
                norm_and_pair(l, 0)
                ffn(l, 0)
                norm_and_pair(l, 1)
                phase_wall(act, "act", walls)
                u = M[("qkv", l)]["u"] - 2
                for j in range(5):
                    round_unit(u + 2 + j)
                for c in range(4):
                    act.wait_ge(rot_used, ROPES * l + 5 + c)
                    nc.scalar.copy(Kh[:, c, :], Kf[:, c, :]).then_inc(part_hi, 1)
                round_unit(u + 2 + 5)
                phase_wall(act, "act", walls)
                diff_attention(l)
                phase_wall(act, "act", walls)
                norm([(cols, 2 * DIFF_HD)] * DIFF_HEADS,
                     [(h % 4, YDh[:, h, :], cols) for h in range(DIFF_HEADS)], nx_d)
                phase_wall(act, "act", walls)
                u = M[("latent", l)]["u"]
                for j in range(3):
                    round_unit(u + 2 + j)
                norm([(cols, Q_RANK), (slice(0, TOK), KV_RANK)],
                     [(c % 4, CNh[:, c, :], cols) for c in range(QC)]
                     + [((QC + c) % 4, CKh[:, c, :], slice(0, TOK)) for c in range(KVC)], nx)
                phase_wall(act, "act", walls)
                for h in range(2):
                    nc.scalar.copy(MK[h][0][64:MLA_QD, :], kr[64:MLA_QD, :]).then_inc(part_hi, 1)
                u = M[("mla", l)]["u"]
                for j in range(2):
                    round_unit(u + 2 + j)
                mla_attention(l)
                phase_wall(act, "act", walls)
                for c in range(4):
                    nc.scalar.copy(YMh[:, c, cols], YM[:, c, cols]).then_inc(part_hi, 1)
                u = M[("four", l)]["u"]
                for j in range(2):
                    round_unit(u + 2 + j)
                k0 = done["four"]
                jobs = [(g, sc_) for g in range(FG) for sc_, _ in streams(both)]
                for t in range(len(jobs) + 1):
                    if t < len(jobs):
                        act.wait_ge(ab_done, k0 + t + 1)
                        if k0 + t >= 2:
                            act.wait_ge(yf_done, k0 + t - 1)
                        nc.scalar.copy(AB[:, t % 2].rearrange("p t n -> p (t n)"), ps[:, 4 + t % 2, :]
                                       ).then_inc(ab_ready, 1)
                    if t >= 1:
                        g, sc_ = jobs[t - 1]
                        act.wait_ge(yf_done, k0 + t)
                        nc.scalar.copy(YFh[:, g, sc_], ps[:, 6 + (t - 1) % 2, 0:SEQ]).then_inc(yf_hi, 1)
                done["four"] += len(jobs)
                phase_wall(act, "act", walls)
                m = M[("merge", l)]
                with loop(act, 2) as i:
                    for j in range(12):
                        u, q = m["u"] + j, m["q"] + j
                        round_unit(u + 2, i, 12, 2)
                        used(u, 0, i, 12)
                        act.wait_ge(psum_free, FREE + q - 1 + i * 12)
                        nc.scalar.activation(sig[:, j % 2, cols], ps[:, 2 * (q % 2), cols], ACT.Sigmoid
                                             ).then_inc(sig_ready, 1)
                act.wait_ge(half_used, 2 * M[("wout", l)]["u"] - 1)
                for c in range(DC):
                    act.wait_ge(merge_ready, FREE + 2 * (m["g"] // NB + c + 1))
                    nc.scalar.copy(xnh[:, c, cols], MG[:, c, cols]).then_inc(yhi_ready, 1)
                down(M[("wout", l)], cols, True)
                norm_and_pair(l, 2)
                ffn(l, 1)
            norm([(LAT, D_MODEL)], [])

        @block.gpsimd
        def _(pool):
            walls, done = [0], dict(norm=0, chunk=0, chain=0)

            def link(ins):
                done["chain"] += 1
                ins.then_inc(pool_chain, 1)
                pool.wait_ge(pool_chain, done["chain"])

            def sum_squares(d, cols, n=DC):
                pool.wait_ge(stat_done, done["norm"])
                link(nc.gpsimd.memset(acc, 0.0))
                with pool.Fori(0, DC // 2) as i:
                    for j in range(2):
                        pool.wait_ge(sq_ready, d + j + 1 + i * 2)
                        pool.wait_ge(acc_ready, FREE + d + j + i * 2)
                        nc.gpsimd.tensor_tensor(acc[:, cols], acc[:, cols], sq[:, j, cols], ALU.add
                                                ).then_inc(acc_ready, 1)

            def lo_chunk(c, dst, hi, cols, src):
                pool.wait_ge(yhi_ready, done["chunk"] + 1 + c)
                nc.gpsimd.tensor_tensor(dst[:, cols], src, hi[:, cols].bitcast(F32), ALU.subtract
                                        ).then_inc(ylo_ready, 1)

            def tile(t, c):
                return t[:, ds(c, 1), :].rearrange("p a n -> p (a n)")

            def x_norm(both):
                cols = width(both)
                done["norm"] += 1
                with pool.Fori(0, DC // 4) as i:
                    for j in range(4):
                        lo_chunk(i * 4 + j, tile(xnl, i * 4 + j), tile(xnh, i * 4 + j), cols, nx[:, j, cols])
                done["chunk"] += DC

            nc.gpsimd.memset(ones[:], 1.0).then_inc(ylo_ready, FREE_NX)
            nc.gpsimd.memset(eps[:], RMS_EPS)
            link(nc.gpsimd.memset(ident[:], 0.0))
            nc.gpsimd.affine_select(out=ident[:], in_=ident[:], compare_op=ALU.not_equal, fill=1.0, base=0,
                                    pattern=[[-1, P]], channel_multiplier=1).then_inc(acc_ready, FREE)
            pool.wait_ge(acc_ready, FREE)
            sum_squares(0, slice(0, TOK))
            for l in range(DEPTH):
                both = l < DEPTH - 1
                cols = width(both)
                x_norm(True)
                sum_squares(M[("down", l, 0, 1)]["d"], slice(0, TOK))
                x_norm(True)
                phase_wall(pool, "pool", walls)
                nc.gpsimd.memset(QM[64:P, :, 0].bitcast(F32), 0.0)
                nc.gpsimd.memset(QM[0:64, :, 1].bitcast(F32), 0.0)
                phase_wall(pool, "pool", walls)
                phase_wall(pool, "pool", walls)
                done["norm"] += 1
                for h in range(DIFF_HEADS):
                    lo_chunk(0, YDl[:, h, :], YDh[:, h, :], cols, nx_d[:, h % 4, cols])
                    done["chunk"] += 1
                phase_wall(pool, "pool", walls)
                done["norm"] += 1
                for c in range(QC + KVC):
                    if c < QC:
                        lo_chunk(0, CNl[:, c, :], CNh[:, c, :], cols, nx[:, c % 4, cols])
                    else:
                        lo_chunk(0, CKl[:, c - QC, :], CKh[:, c - QC, :], slice(0, TOK), nx[:, c % 4, :])
                    done["chunk"] += 1
                phase_wall(pool, "pool", walls)
                phase_wall(pool, "pool", walls)
                phase_wall(pool, "pool", walls)
                done["chunk"] += DC
                sum_squares(M[("wout", l)]["d"], cols)
                x_norm(both)
                sum_squares(M[("down", l, 1, 1)]["d"], cols)

        @block.vector
        def _(dve):
            walls, done = [0], dict(norm=0, group=0, chunk=0, item=0, pair=0, part=0, head=0, qhead=0, four=0,
                                    chain=0, rot=0, y=0)

            def link(ins):
                done["chain"] += 1
                ins.then_inc(dve_chain, 1)
                dve.wait_ge(dve_chain, done["chain"])

            def split_half(u, h, i=0, per=0, n=1):
                if u >= len(UNITS):
                    return
                w = ahead(u, per, n)[h]
                dve.wait_ge(hi_ready, 2 * u + h + 1 + i * (2 * per))
                nc.vector.tensor_tensor(wl[:, u % 2, h, 0:w], raw[:, u % RAW, h, 0:w],
                                        wh[:, u % 2, h, 0:w].bitcast(F32), ALU.subtract).then_inc(split_ready, 1)

            def split_unit(u, i=0, per=0, n=1):
                for h in range(2):
                    split_half(u, h, i, per, n)

            def used(u, h, i=0, per=0):
                dve.wait_ge(half_used, 2 * u + h + 1 + i * (2 * per))

            def tile(t, c):
                return t[:, c, :] if isinstance(c, int) else t[:, ds(c, 1), :].rearrange("p a n -> p (a n)")

            def ada_vectors(a, i=0):
                dve.wait_ge(ada_turned, a + 1 + i)
                dve.wait_ge(mods_ready, a + i)
                nc.vector.tensor_reduce(ada_sum[:].rearrange("p (c e) -> p c e", c=2),
                                        ps[:, B_T, 0:144].rearrange("p (c e z) -> p c e z", c=2, z=2)[:, :, 0:4, :],
                                        axis=AX_X, op=ALU.add).then_inc(ada_summed, 1)
                dve.wait_ge(ada_summed, a + 1 + i)
                t = slice(4 * a, 4 * a + 4) if isinstance(i, int) else ds(i * 4 + 4 * a, 4)
                out = mods[:, :, t].rearrange("p v (u c) -> p c u v", c=2)
                bias = adab[:, t].rearrange("p (u c) -> p c u", c=2)
                for v_ in range(2):
                    ins = nc.vector.tensor_tensor(out[:, :, :, v_],
                                                  ada_sum[:].rearrange("p (c u v) -> p c u v", c=2, u=2)[:, :, :, v_],
                                                  bias, ALU.add)
                ins.then_inc(mods_ready, 1)

            def norm(groups, tmp):
                done["norm"] += 1
                dve.wait_ge(std_ready, done["norm"])
                n = sum((cols.stop - cols.start) // P for cols, _ in groups)
                nc.vector.reciprocal(rs[:, 0:n], sd[:, 0:n]).then_inc(rstd_ready, 1)
                k = 0
                for cols, chunks in groups:
                    dve.wait_ge(rb_ready, done["group"] + 1)
                    row = ps[:, (B_RB, B_ADA)[done["group"] % 2], cols]
                    if callable(chunks):
                        with dve.Fori(0, DC // 4) as i:
                            for j in range(5):
                                if j < 4:
                                    by_rstd(j, row, cols, i * 4 + j, tmp, *chunks(i * 4 + j))
                                if j:
                                    scaled(j - 1, i * 4 + j - 1, tmp, *chunks(i * 4 + j - 1))
                        done["chunk"] += DC
                        done["y"] += DC
                    else:
                        for c in range(len(chunks) + 1):
                            if c < len(chunks):
                                by_rstd((k + c) % 4, row, cols, c, tmp, *chunks[c])
                            if c:
                                scaled((k + c - 1) % 4, c - 1, tmp, *chunks[c - 1])
                        k += len(chunks)
                        done["chunk"] += len(chunks)
                        done["y"] += len(chunks)
                    done["group"] += 1
                    dve.drain().then_inc(rb_used, 1)

            def by_rstd(b, row, cols, c, tmp, src, by_stream, dst=None):
                if dst is None:
                    dve.wait_ge(ylo_ready, FREE_NX + done["chunk"] - 3 + c)
                nc.vector.tensor_tensor(tmp[:, b, cols], src[:, cols], row, ALU.mult).then_inc(nt_ready, 1)

            def scaled(b, c, tmp, src, by_stream, dst=None):
                dve.wait_ge(nt_ready, done["y"] + 1 + c)
                for st, scale, shift in by_stream:
                    out = tmp[:, b, st] if dst is None else dst
                    if shift is None:
                        ins = nc.vector.tensor_scalar(out, tmp[:, b, st], scale, None, ALU.mult)
                    else:
                        ins = nc.vector.tensor_scalar(out, tmp[:, b, st], scale, shift, ALU.mult, ALU.add)
                ins.then_inc(y_ready, 1)

            def norm_scale(l, k):
                both = l < DEPTH - 1 or k < 2
                t0 = l * MODT + 3 * k * DC
                dve.wait_ge(mods_ready, (t0 + 2 * DC) // 4)
                for _, s_ in streams(both):
                    link(nc.vector.tensor_scalar(amul[:, s_, :], mods[:, s_, t0 + DC:t0 + 2 * DC], 1.0, None, ALU.add))
                    link(nc.vector.tensor_tensor(amul[:, s_, :], amul[:, s_, :],
                                                 gains[:, (l * 3 + k) * DC:(l * 3 + k + 1) * DC], ALU.mult))

            def x_norm(l, k):
                both = l < DEPTH - 1 or k < 2
                t0 = l * MODT + 3 * k * DC

                def chunk(c):
                    return (tile(x, c), [(st, amul[:, s_, ds(c, 1)], mods[:, s_, ds(c + t0, 1)])
                                         for st, s_ in streams(both)])

                norm([(width(both), chunk)], nx)

            def gate(l, k, half_it, both):
                t0 = l * MODT + (3 * k + 2) * DC
                dve.wait_ge(mods_ready, (t0 + DC) // 4)
                for _, s_ in streams(both):
                    link(nc.vector.tensor_scalar(ghalf[:, s_, :], mods[:, s_, t0:t0 + DC], 0.5 if half_it else 1.0,
                                                 None, ALU.mult))

            def down(m, both):
                dve.wait_ge(psum_free, FREE + m["q"])
                end = m["u"] + DC >= len(UNITS)
                for first, n in ([(0, 1), (4, 1)] if end else [(0, DC // 4)]):
                    with loop(dve, n) as i:
                        for j in range(first, first + 4):
                            u, q = m["u"] + j, m["q"] + j
                            split_half(u + 2, 0, i, 4, n)
                            used(u, 1, i, 4)
                            c = i * 4 + j
                            for st, s_ in streams(both):
                                g = ghalf[:, s_, c:c + 1] if isinstance(c, int) else ghalf[:, s_, ds(c, 1)]
                                xt = tile(x, c)[:, st]
                                ins = nc.vector.scalar_tensor_tensor(out=xt, in0=ps[:, 2 * (q % 2), st], scalar=g,
                                                                     in1=xt, op0=ALU.mult, op1=ALU.add)
                            ins.then_inc(psum_free, 1)
                            split_half(u + 2, 1, i, 4, n)

            def norm_and_pair(l, k):
                m = M[("pre", l, k)]
                norm_scale(l, k)
                if m["ada"]:
                    split_unit(m["u"] + 2)
                    split_unit(m["u"] + 3)
                x_norm(l, k)
                if m["ada"]:
                    ada_vectors(m["a"])

            def hidden(u, q, f, fl, cols, i=0, per=0, jobs=0, n=1):
                b = f % 2
                split_half(u + 2, 0, i, per, n)
                dve.wait_ge(silu_ready, f + 1 + i * jobs)
                used(u, 1, i, per)
                dve.wait_ge(h_ready, FREE + f - 1 + i * jobs)
                nc.vector.tensor_tensor(ht[:, b, cols], sil[:, b, cols], ps[:, 2 * (q % 2) + 1, cols], ALU.mult
                                        ).then_inc(psum_free, 1)
                split_half(u + 2, 1, i, per, n)
                dve.wait_ge(hhi_ready, f + 1 + i * jobs)
                fl = i * jobs + fl
                nc.vector.tensor_tensor(tile(hl, fl)[:, cols], ht[:, b, cols], tile(hh, fl)[:, cols].bitcast(F32),
                                        ALU.subtract).then_inc(h_ready, 1)

            def ffn(l, k):
                both = l < DEPTH - 1 or k == 0
                cols = width(both)
                pre = M[("pre", l, 2 * k)]
                for j in range(2):
                    hidden(pre["u"] + 2 * pre["ada"] + j, pre["q"] + j, pre["f"] + j, j, cols)
                for part, nf in enumerate(F_HALVES):
                    for u0, q0, f0, a0, body, n in up_runs(l, k, part):
                        per, jobs = len(body), body.count("up")
                        fl0 = f0 - (pre["f"] if part == 0 else M[("up", l, k, part)]["f"])
                        with loop(dve, n) as i:
                            j = 0
                            for p, kind in enumerate(body):
                                u = u0 + p
                                if kind == "ada":
                                    split_unit(u + 2, i, per, n)
                                    continue
                                hidden(u, q0 + j, f0 + j, fl0 + j, cols, i, per, jobs, n)
                                j += 1
                            if a0 is not None:
                                ada_vectors(a0, i)
                    if part == 0:
                        gate(l, 2 * k, True, both)
                    down(M[("down", l, k, part)], both)

            def evacuate(q, copies):
                for dst, src in copies[:-1]:
                    nc.vector.tensor_copy(dst, src)
                nc.vector.tensor_copy(*copies[-1]).then_inc(psum_free, 1)

            def values(u, q, col):
                used(u, 1)
                evacuate(q, [(Vt[:, 2 * b:2 * b + 2, col:col + 256],
                              ps[:, 2 * (q % 2) + b, :].rearrange("p (t n) -> p t n", t=2)) for b in range(2)])

            def rope(rows, src, rot, table, tmp, signal):
                done["rot"] += 1
                dve.wait_ge(rot_done, done["rot"])
                nc.vector.tensor_tensor(tmp, rot, table[rows, 1, :], ALU.mult)
                link(nc.vector.tensor_tensor(src, src, table[rows, 0, :], ALU.mult))
                nc.vector.tensor_tensor(src, src, tmp, ALU.add).then_inc(*signal)

            def negmax(a, banks, scale, nk):
                dve.wait_ge(qk_done, a + 1)
                n = len(banks)
                for m, bank in enumerate(banks):
                    ins = nc.vector.reduce_max(mx[:, a % 2, m:m + 1], ps[:, bank, 0:nk], AX_X)
                link(ins)
                nc.vector.tensor_scalar(nm[:, a % 2, 0:n], mx[:, a % 2, 0:n], -scale, None, ALU.mult
                                        ).then_inc(negmax_ready, 1)

            def diff_weights(a, l, t, nk):
                dve.wait_ge(exp_done, a + 1)
                b = a % 2
                link(nc.vector.reciprocal(rr[:, b, :], sm[:, b, :]))
                link(nc.vector.tensor_scalar(rr[:, b, 1:2], rr[:, b, 1:2], nlam[:, l:l + 1], None, ALU.mult))
                p0, p1 = Pd[:, t % 2, 0, 0:nk], Pd[:, t % 2, 1, 0:nk]
                link(nc.vector.tensor_scalar(p1, p1, rr[:, b, 1:2], None, ALU.mult))
                nc.vector.scalar_tensor_tensor(out=p0, in0=p0, scalar=rr[:, b, 0:1], in1=p1, op0=ALU.mult, op1=ALU.add
                                               ).then_inc(w_ready, 1)

            def mla_weights(a, t, nk):
                dve.wait_ge(exp_done, a + 1)
                b = a % 2
                link(nc.vector.reciprocal(rr[:, b, 0:1], sm[:, b, 0:1]))
                p = Pm[:, t % 2, 0:nk]
                nc.vector.tensor_scalar(p, p, rr[:, b, 0:1], None, ALU.mult).then_inc(w_ready, 1)

            def take_output(g, dst, rows):
                dve.wait_ge(pv_done, g + 1)
                nc.vector.tensor_copy(dst, ps[rows, B_O, 0:256]).then_inc(o_ready, 1)

            def diff_q(l, h):
                cols = width(l < DEPTH - 1)
                done["qhead"] += 1
                dve.wait_ge(qhi_ready, done["qhead"])
                for m, rows in enumerate((slice(0, 64), slice(64, P))):
                    ins = nc.vector.tensor_tensor(QM[rows, h % 2, m, 1, cols], Qf[rows, h, cols],
                                                  QM[rows, h % 2, m, 0, cols].bitcast(F32), ALU.subtract)
                ins.then_inc(q_ready, 1)

            def diff_attention(l):
                items, pairs = item_list(l, DIFF_HEADS)
                a0, g0 = done["item"], done["pair"]
                diff_q(l, 0)
                for t in range(len(items) + 3):
                    if t < len(items):
                        h, g, _, col, nk = items[t]
                        negmax(a0 + t, (2 * (t % 2), 2 * (t % 2) + 1), DIFF_HD ** -0.5, nk)
                        if (t == 0 or items[t - 1][0] != h) and h + 1 < DIFF_HEADS:
                            diff_q(l, h + 1)
                    if 1 <= t <= len(items):
                        diff_weights(a0 + t - 1, l, t - 1, items[t - 1][4])
                    if t >= 3 and items[t - 3][2] == 1:
                        h, g = items[t - 3][:2]
                        take_output(g0 + g, Qf[:, h, pairs[g][1]], slice(0, P))
                done["item"] += len(items)
                done["pair"] += len(pairs)

            def rope_rows(out, rope_psum, rotated_psum):
                link(nc.vector.tensor_tensor(rope_t[64:MLA_QD, :], rotated_psum, rope_m[MLA_QD:P, 1, :], ALU.mult))
                link(nc.vector.tensor_tensor(out, rope_psum, rope_m[64:MLA_QD, 0, :], ALU.mult))
                return nc.vector.tensor_tensor(out, out, rope_t[64:MLA_QD, :], ALU.add)

            def mla_rope(l, h):
                m = M[("mla", l)]
                u, q = m["u"] + 2 + 2 * (h // 2), m["q"] + 2 + 2 * (h // 2)
                bank = ps[:, 2 * (q % 2) + h % 2, LAT]
                used(u, h % 2)
                rope_rows(bank[64:MLA_QD], bank[64:MLA_QD], bank[MLA_QD:P]).then_inc(mq_ready, 1)

            def mla_qk(l, h):
                m = M[("mla", l)]
                cols = width(l < DEPTH - 1)
                j, q = h % 2, m["q"] + 2 + 2 * (h // 2)
                done["qhead"] += 1
                dve.wait_ge(qhi_ready, done["qhead"])
                nc.vector.tensor_tensor(MQ[0:MLA_QD, j, 1, cols], ps[0:MLA_QD, 2 * (q % 2) + j, cols],
                                        MQ[0:MLA_QD, j, 0, cols].bitcast(F32), ALU.subtract)
                nc.vector.tensor_tensor(MK[j][1][0:64, :], ps[0:64, 2 * ((q + 1) % 2) + j, :],
                                        MK[j][0][0:64, :].bitcast(F32), ALU.subtract).then_inc(q_ready, 1)
                if j:
                    dve.drain().then_inc(psum_free, 2)

            def mla_split(l, i, p):
                split_half(M[("mla", l)]["u"] + 2 + 2 * i + p // 2 + 2, p % 2)

            def mla_attention(l):
                items, pairs = item_list(l, MLA_HEADS)
                a0, g0 = done["item"], done["pair"]
                for p in range(4):
                    mla_split(l, 0, p)
                for h in range(2):
                    mla_rope(l, h)
                    mla_qk(l, h)
                for t in range(len(items) + 3):
                    head, halves = mla_extras(l, t) if t < len(items) else (None, [])
                    if head is not None:
                        mla_rope(l, head)
                    if t < len(items):
                        negmax(a0 + t, (B_S + t % 2,), MLA_QD ** -0.5, items[t][4])
                    if 1 <= t <= len(items):
                        mla_weights(a0 + t - 1, t - 1, items[t - 1][4])
                    if t >= 3 and items[t - 3][2] == 1:
                        h, g = items[t - 3][:2]
                        rows = slice(64 * (h % 2), 64 * (h % 2) + 64)
                        take_output(g0 + g, YM[rows, h // 2, pairs[g][1]], rows)
                    if head is not None:
                        mla_qk(l, head)
                    for i, p in halves:
                        mla_split(l, i, p)
                done["item"] += len(items)
                done["pair"] += len(pairs)

            def sum_of_squares(dst, chunks, tmp):
                for n, c in enumerate(chunks):
                    o = dst if n == 0 else tmp
                    link(nc.vector.tensor_tensor(o, c, c, ALU.mult))
                    if n:
                        link(nc.vector.tensor_tensor(dst, dst, tmp, ALU.add))

            link(nc.vector.memset(cz[:].bitcast(F32), 0.0))
            nc.vector.memset(rs[:], 0.0).then_inc(psum_free, FREE)
            nc.vector.memset(sd[:], 0.0).then_inc(h_ready, FREE)
            nc.vector.memset(mx[:], 0.0).then_inc(rb_used, FREE)
            nc.vector.memset(nlam[:], 0.0).then_inc(merge_ready, FREE)
            dve.wait_ge(act_chain, 2)
            nc.vector.tensor_tensor(cz[:, :, 5:8:2], vsil[:], cz[:, :, 4:8:2].bitcast(F32), ALU.subtract
                                    ).then_inc(setup_ready, 1)
            split_unit(0)
            split_unit(1)
            dve.wait_ge(c_loaded, 32)
            for a in range(4):
                split_unit(2 * a + 2)
                split_unit(2 * a + 3)
                ada_vectors(a)
            dve.wait_ge(consts_loaded, 16 * 8)
            lam4 = SD[:, 0:512].rearrange("p (l a b d) -> p l a b d", l=DEPTH, a=2, b=2)
            lamt = SD[:, 512:768].rearrange("p (l a d) -> p l a d", l=DEPTH, a=2)
            for l in range(DEPTH):
                link(nc.vector.tensor_tensor(lamt[:, l], lam4[:, l, :, 0], lam4[:, l, :, 1], ALU.mult))
            link(nc.vector.tensor_reduce(lamp[:], lamt, axis=AX_X, op=ALU.add))
            assert done["chain"] == DVE_LAM
            dve.wait_ge(act_chain, 3)
            for l in range(DEPTH):
                link(nc.vector.tensor_tensor(nlam[:, l:l + 1], lamp[:, l, 1:2], lamp[:, l, 0:1], ALU.subtract))
                link(nc.vector.tensor_scalar(nlam[:, l:l + 1], nlam[:, l:l + 1], -LAM_INIT[l], None, ALU.add))
                link(nc.vector.tensor_scalar(gsub[:, l:l + 1], gsub[:, l:l + 1], 1.0 - LAM_INIT[l], None, ALU.mult))

            for l in range(DEPTH):
                both = l < DEPTH - 1
                cols = width(both)
                norm_and_pair(l, 0)
                ffn(l, 0)
                norm_and_pair(l, 1)
                phase_wall(dve, "dve", walls)
                m = M[("qkv", l)]
                u, q = m["u"] - 2, m["q"] - 2
                for j in range(4):
                    split_unit(u + 2 + j)
                    used(u + j, 1)
                    c_, dst = (cols, Qf) if j < 2 else (slice(0, TOK), Kf)
                    evacuate(q + j, [(dst[:, 2 * (j % 2) + b, c_], ps[:, 2 * ((q + j) % 2) + b, c_]) for b in range(2)])
                for c in range(8):
                    src = (Qf if c < 4 else Kf)[:, c % 4, LAT]
                    rope(slice(0, P), src, ps[:, 4 + c % 2, 0:SEQ], rope_d, SD[:, 256 * (c % 2):256 * (c % 2) + 256],
                         (rot_used, 1))
                    if c == 3:
                        split_unit(u + 2 + 4)
                        values(u + 4, q + 4, 0)
                    if c >= 4:
                        done["part"] += 1
                        dve.wait_ge(part_hi, done["part"])
                        nc.vector.tensor_tensor(Kl[:, c - 4, :], Kf[:, c - 4, :], Kh[:, c - 4, :].bitcast(F32),
                                                ALU.subtract).then_inc(part_lo, 1)
                split_unit(u + 2 + 5)
                values(u + 5, q + 5, 256)
                phase_wall(dve, "dve", walls)
                diff_attention(l)
                phase_wall(dve, "dve", walls)
                for h in range(DIFF_HEADS):
                    ins = nc.vector.tensor_tensor(head_squares(h)[:, cols], Qf[:, h, cols], Qf[:, h, cols], ALU.mult)
                ins.then_inc(part_lo, 1)
                norm([(cols, [(Qf[:, h, :], [(cols, gsub[:, l:l + 1], None)])]) for h in range(DIFF_HEADS)],
                     nx_d)
                phase_wall(dve, "dve", walls)
                m = M[("latent", l)]
                u, q = m["u"], m["q"]
                for j in range(3):
                    split_unit(u + 2 + j)
                    used(u + j, 1)
                    b = 2 * ((q + j) % 2)
                    c0_, c1_ = (cols if j < 2 else slice(0, TOK)), (cols if j < 1 else slice(0, TOK))
                    if j < 2:
                        evacuate(q + j, [(CQ[:, 2 * j, c0_], ps[:, b, c0_]), (CQ[:, 2 * j + 1, c1_], ps[:, b + 1, c1_])])
                        if j == 1:
                            dve.wait_ge(psum_free, FREE + q + 2)
                            sum_of_squares(SB[:, cols], [CQ[:, c, cols] for c in range(QC)],
                                           SB[:, 1024:1024 + cols.stop - cols.start])
                        continue
                    nc.vector.tensor_copy(CQ[:, 4, :], ps[:, b, :])
                    rope_rows(kr[64:MLA_QD, LAT], ps[64:MLA_QD, b + 1, LAT], ps[MLA_QD:P, b + 1, LAT])
                    evacuate(q + j, [(kr[64:MLA_QD, CTX], ps[64:MLA_QD, b + 1, CTX])])
                sum_of_squares(SB[:, 512:1024], [CQ[:, QC + c, :] for c in range(KVC)], SB[:, 1024:1536])
                dve.drain().then_inc(part_lo, 1)
                norm([(cols, [(CQ[:, c, :], [(cols, gq[:, l * QC + c:l * QC + c + 1], None)])
                              for c in range(QC)]),
                      (slice(0, TOK), [(CQ[:, QC + c, :], [(slice(0, TOK), gkv[:, l * KVC + c:l * KVC + c + 1], None)])
                                       for c in range(KVC)])], nx)
                phase_wall(dve, "dve", walls)
                for h in range(2):
                    done["part"] += 1
                    dve.wait_ge(part_hi, done["part"])
                    nc.vector.tensor_tensor(MK[h][1][64:MLA_QD, :], kr[64:MLA_QD, :],
                                            MK[h][0][64:MLA_QD, :].bitcast(F32), ALU.subtract).then_inc(part_lo, 1)
                dve.wait_ge(part_lo, PARTS * l + 8)
                m = M[("mla", l)]
                for j in range(2):
                    split_unit(m["u"] + 2 + j)
                    values(m["u"] + j, m["q"] + j, 256 * j)
                mla_attention(l)
                phase_wall(dve, "dve", walls)
                for c in range(4):
                    done["part"] += 1
                    dve.wait_ge(part_hi, done["part"])
                    nc.vector.tensor_tensor(YMl[:, c, cols], YM[:, c, cols], YMh[:, c, cols].bitcast(F32),
                                            ALU.subtract).then_inc(part_lo, 1)
                m = M[("four", l)]
                for j in range(2):
                    split_unit(m["u"] + 2 + j)
                    used(m["u"] + j, 1)
                    q = m["q"] + j
                    evacuate(q, [(Ff[:, 2 * j + b, cols], ps[:, 2 * (q % 2) + b, cols]) for b in range(2)])
                jobs = [(g, sc_) for g in range(FG) for sc_, _ in streams(both)]
                for t, (g, sc_) in enumerate(jobs):
                    done["four"] += 1
                    dve.wait_ge(yf_hi, done["four"])
                    nc.vector.tensor_tensor(YFl[:, g, sc_], ps[:, 6 + t % 2, 0:SEQ], YFh[:, g, sc_].bitcast(F32),
                                            ALU.subtract).then_inc(yf_ready, 1)
                phase_wall(dve, "dve", walls)
                m = M[("merge", l)]
                with loop(dve, 2) as i:
                    for j in range(12):
                        u, q, b = m["u"] + j, m["q"] + j, j % NB
                        mm = i * 4 + j // NB
                        n_add = 2 * (m["g"] // NB) + 2 * (j // NB) + i * 8
                        split_unit(u + 2, i, 12, 2)
                        dve.wait_ge(sig_ready, m["g"] + j + 1 + i * 12)
                        used(u, 1, i, 12)
                        s_, y_ = sig[:, j % 2, cols], ps[:, 2 * (q % 2) + 1, cols]
                        dst = tile(MG, mm)[:, cols]
                        if b == 0:
                            nc.vector.tensor_tensor(dst, s_, y_, ALU.mult).then_inc(psum_free, 1)
                        else:
                            dve.wait_ge(merge_ready, FREE + n_add)
                            nc.vector.tensor_tensor(prod[:, b - 1, cols], s_, y_, ALU.mult).then_inc(psum_free, 1)
                            dve.wait_ge(psum_free, FREE + q + 1 + i * 12)
                            dve.wait_ge(merge_ready, FREE + n_add + b - 1)
                            nc.vector.tensor_tensor(dst, dst, prod[:, b - 1, cols], ALU.add).then_inc(merge_ready, 1)
                for c in range(DC):
                    done["chunk"] += 1
                    dve.wait_ge(yhi_ready, done["chunk"])
                    nc.vector.tensor_tensor(xnl[:, c, cols], MG[:, c, cols], xnh[:, c, cols].bitcast(F32),
                                            ALU.subtract).then_inc(ylo_ready, 1)
                gate(l, 1, False, both)
                down(M[("wout", l)], both)
                norm_and_pair(l, 2)
                ffn(l, 1)
            norm([(LAT, [(x[:, c, :], [(LAT, gfin[:, c:c + 1], None)], out_y[:, c, :]) for c in range(DC)])], nx)
    return nc



def _rows(w):
    return w.reshape(-1, P, w.shape[-1]).transpose(1, 0, 2)


def _cols(v_):
    return np.ascontiguousarray(v_.reshape(-1, P).T)


ROTATED = np.arange(MLA_ROPE).reshape(2, 2, -1)[:, ::-1].reshape(-1)
HEAD_COLS = np.concatenate([np.arange(MLA_QD), MLA_NOPE + ROTATED])


def _tables():
    def rope(dim):
        nf = dim // 4
        freqs = np.power(np.float32(ROPE_BASE), -np.arange(nf, dtype=np.float32) / nf)
        t = np.arange(SEQ)
        ar = (t // GRID_W).astype(np.float32)[:, None] * freqs
        ac = (t % GRID_W).astype(np.float32)[:, None] * freqs
        ang = np.concatenate([ar, ar, ac, ac], -1).T
        return np.stack([np.cos(ang), np.sin(ang)], 1).astype(np.float32)

    def rotation(n, dim, first):
        r, q = np.zeros((n, n), np.float32), dim // 4
        for base in range(first, n, dim):
            for m in range(dim):
                if (m // q) % 2 == 0:
                    r[base + m + q, base + m] = -1.0
                else:
                    r[base + m - q, base + m] = 1.0
        return r

    rope_d = np.concatenate([rope(DIFF_HD)] * 2)
    rope_m = np.zeros((P, 2, SEQ), np.float32)
    rope_m[MLA_NOPE:MLA_QD, 0] = rope(MLA_ROPE)[:, 0]
    sign = np.where(np.arange(MLA_ROPE) // (MLA_ROPE // 4) % 2 == 0, -1, 1).astype(np.float32)
    rope_m[MLA_QD:, 1] = rope(MLA_ROPE)[:, 1] * sign[:, None]
    k, n = np.arange(P), np.arange(SEQ)
    ang_d = 2 * np.pi * (np.outer(k, k) % P) / P
    ang_n = 2 * np.pi * (np.outer(n, n) % SEQ) / SEQ
    s = (SEQ * P) ** -0.5
    cn, sn = (f(ang_n).reshape(2, P, SEQ).transpose(1, 0, 2).reshape(P, 2 * SEQ) for f in (np.cos, np.sin))
    dft = np.concatenate([np.cos(ang_d) * s, np.sin(ang_d) * s, cn, -sn], 1).astype(np.float32)
    return dict(rope_d=rope_d, rope_m=rope_m, rot_d=rotation(P, DIFF_HD, 0),
                dft=dft)


def _pack(I):
    out = {k: [] for k in KINDS}

    def put(kind, *halves):
        out[kind].append(np.concatenate([h.reshape(P, -1) for h in halves], 1))

    for l in range(DEPTH):
        w = _rows(I["ada_w"][l])
        for c in range(0, N_MOD * D_MODEL, 256):
            put("ada", w[:, :, c:c + 256])
        for k in range(2):
            w = _rows(I["ffn_w_in"][l, k])
            for c in range(0, D_FF, P):
                put("up", w[:, :, c:c + P], w[:, :, D_FF + c:D_FF + c + P])
            w, c0 = _rows(I["ffn_w_out"][l, k]), 0
            for part, nf in enumerate(F_HALVES):
                for m in range(0, D_MODEL, P):
                    put(f"dn{part}", w[:, c0:c0 + nf, m:m + P])
                c0 += nf
        w = _rows(I["w_in"][l])
        o = [int(v_) for v_ in IN_OFF]

        def tiles(c):
            put("proj", w[:, :, c:c + P], w[:, :, c + P:c + 2 * P])

        for c in (0, 256, 512, 768):
            tiles(c)
        for c in (0, 256):
            put("proj", w[:, :, o[2] + c:o[2] + c + 256])
        for c in (0, 256):
            tiles(o[3] + c)
        put("kr", w[:, :, o[5] - P:o[5]],
            np.concatenate([w[:, :, o[5] - MLA_NOPE:o[6]], w[:, :, o[5] + ROTATED]], -1))
        for c in (0, 256):
            tiles(o[6] + c)
        wq = _rows(I["mla_w_uq"][l])
        wkv = _rows(I["mla_w_ukv"][l]).reshape(P, KVC, MLA_HEADS, P)
        for h in (0, 4):
            put("kvv", wkv[:, :, h:h + 4, MLA_NOPE:])
        for h in range(0, MLA_HEADS, 2):
            put("uq", *(wq[:, :, (h + j) * MLA_QD + HEAD_COLS] for j in range(2)))
            put("kvk", *(wkv[:, :, h + j] for j in range(2)))
        wb = [_rows(I[n][l]) for n in ("w_branch_diff", "w_branch_mla", "w_branch_fourier")]
        wo = _rows(I["w_out"][l])
        for m in range(0, D_MODEL, P):
            for b in range(NB):
                c = o[7] + b * D_MODEL + m
                put("merge", w[:, :, c:c + P], wb[b][:, :, m:m + P])
            put("wout", wo[:, :, m:m + P])
    return {k: np.stack(v_) for k, v_ in out.items()}


def kernel(**inputs):
    import numpy as _np
    import concourse.bacc as _bacc
    from concourse.bass_utils import run_bass_kernel_spmd as _run

    I = {k: _np.asarray(v_) for k, v_ in inputs.items()}
    arrays = dict(_pack(I), **_tables())
    arrays["xT"] = I["x"][0].T.reshape(DC, P, SEQ).transpose(1, 0, 2)
    arrays["ctxT"] = I["ctx"][0].T.reshape(DC, P, CTX_LEN).transpose(1, 0, 2)
    arrays["vec"] = _np.stack([I["c"][0].reshape(DC, P), I["c_ctx"].reshape(DC, P)], -1).transpose(1, 0, 2)
    arrays["ada_b"] = _cols(I["ada_b"])
    arrays["norm_g"] = _cols(I["norm_g"])
    arrays["final_g"] = _cols(I["final_norm_g"])
    arrays["sub_g"] = _cols(I["diff_subln_g"])
    arrays["q_g"] = _cols(I["mla_q_norm_g"])
    arrays["kv_g"] = _cols(I["mla_kv_norm_g"])
    arrays["lam"] = _np.broadcast_to(I["diff_lambda"].reshape(1, -1), (P, DEPTH * 4 * DIFF_HD))
    arrays = {f"in_{k}": _np.ascontiguousarray(v_) for k, v_ in arrays.items()}

    nc = _bacc.Bacc("TRN2", target_bir_lowering=False, num_devices=1)
    A = {k[3:]: nc.dram_tensor(k, v_.shape, F32, kind="ExternalInput").ap() for k, v_ in arrays.items()}
    A["out"] = nc.dram_tensor("out", (P, DC, SEQ), F32, kind="ExternalOutput").ap()
    build(nc, A)
    r = _run(nc, [arrays], core_ids=[0])
    got = r.results[0]["out"]
    return got.transpose(2, 1, 0).reshape(1, SEQ, D_MODEL)
```
